# Optimizing a Trainium2 kernel written in Bass

```python
import math
import jax
import jax.numpy as jnp
from jax import lax
import numpy as np

D_MODEL = 1024
BATCH = 1
SEQ = 1024
DEPTH = 1
DEC_BATCH = 8
DEC_SEQ = 4
PAST_LEN = 8192
PAGE_SIZE = 128

DN_HEADS = 6
DN_DK = 64
DN_DV = 64
DN_QK = DN_HEADS * DN_DK
DN_WIDTH = DN_HEADS * DN_DV
CONV_W = 4
ML_HEADS = 6
ML_DK = 64
ML_DV = 64
ML_QK = ML_HEADS * ML_DK
ML_WIDTH = ML_HEADS * ML_DV
S5_WIDTH = D_MODEL - DN_WIDTH - ML_WIDTH
S5_GROUP = 16
S5_GROUPS = S5_WIDTH // S5_GROUP
S5_P = 64
N_MEM = 256
X_HEADS = 4
X_HD = 128
X_WIDTH = X_HEADS * X_HD
D_FF = 4 * D_MODEL
CHUNK = 64
EPS = 1e-6
IN_SIZES = (DN_QK, DN_QK, DN_WIDTH, DN_HEADS, DN_HEADS, DN_WIDTH,
            ML_QK, ML_QK, ML_WIDTH, ML_HEADS, ML_HEADS, ML_WIDTH, S5_WIDTH)
P_IN = 2 * DN_QK + 2 * DN_WIDTH + 2 * DN_HEADS + 2 * ML_QK + 2 * ML_WIDTH + 2 * ML_HEADS + S5_WIDTH
CONV_CH = 2 * DN_QK + DN_WIDTH

kernel_name = 'hybrid_deltanet_mlstm_s5_decoder_step'

def _split_points():
    return [int(s) for s in np.cumsum(IN_SIZES)[:-1]]

def rmsnorm(x, g):
    xf = x.astype(jnp.float32)
    y = xf * lax.rsqrt(jnp.mean(xf * xf, axis=-1, keepdims=True) + EPS)
    return (y * g.astype(jnp.float32)).astype(x.dtype)

def _l2norm(t):
    t = t.astype(jnp.float32)
    return t * lax.rsqrt(jnp.sum(t * t, axis=-1, keepdims=True) + EPS)

def _chunk_len(L):
    return L if L <= CHUNK else math.gcd(L, CHUNK)

def _to_blocks(t, c):
    b, l, h = t.shape[:3]
    t = t.astype(jnp.float32).reshape((b, l // c, c, h) + t.shape[3:])
    return jnp.moveaxis(t, (1, 3), (0, 2))

def _from_blocks(t):
    t = jnp.moveaxis(t, (0, 2), (1, 3))
    return t.reshape((t.shape[0], t.shape[1] * t.shape[2]) + t.shape[3:])

def causal_conv_silu(u, buf, w):
    L = u.shape[1]
    ext = jnp.concatenate([buf.astype(u.dtype), u], axis=1)
    out = ext[:, 0:L] * w[0]
    for j in range(1, CONV_W):
        out = out + ext[:, j:j + L] * w[j]
    return jax.nn.silu(out), ext[:, L:]

def gated_delta_rule(q, k, v, g, beta, s0):
    dk = q.shape[-1]
    dv = v.shape[-1]
    c = _chunk_len(q.shape[1])
    q = _to_blocks(q, c) * (dk ** -0.5)
    k = _to_blocks(k, c)
    v = _to_blocks(v, c)
    g = _to_blocks(g, c)
    beta = _to_blocks(beta, c)
    G = jnp.cumsum(g, axis=-1)
    incl = jnp.tril(jnp.ones((c, c), dtype=bool))
    strict = jnp.tril(jnp.ones((c, c), dtype=bool), -1)
    decay = jnp.exp(jnp.where(incl, G[..., :, None] - G[..., None, :], -jnp.inf))
    kb = k * beta[..., None]
    m_low = jnp.where(strict, jnp.einsum('nbhik,nbhjk->nbhij', kb, k) * decay, 0.0)
    rhs = jnp.concatenate([v * beta[..., None], kb * jnp.exp(G)[..., None]], axis=-1)
    sol = lax.linalg.triangular_solve(m_low + jnp.eye(c, dtype=jnp.float32), rhs,
                                      left_side=True, lower=True, unit_diagonal=True)
    u_blk, w_blk = sol[..., :dv], sol[..., dv:]
    a_in = jnp.where(incl, jnp.einsum('nbhik,nbhjk->nbhij', q, k) * decay, 0.0)

    def step(S, xs):
        qc, kc, uc, wc, Gc, ac = xs
        v_new = uc - jnp.einsum('bhck,bhkv->bhcv', wc, S)
        o = (jnp.einsum('bhck,bhkv->bhcv', qc * jnp.exp(Gc)[..., None], S)
             + jnp.einsum('bhij,bhjv->bhiv', ac, v_new))
        g_last = Gc[..., -1]
        S = (S * jnp.exp(g_last)[..., None, None]
             + jnp.einsum('bhck,bhcv->bhkv', kc * jnp.exp(g_last[..., None] - Gc)[..., None], v_new))
        return S, o

    S, o = lax.scan(step, s0.astype(jnp.float32), (q, k, u_blk, w_blk, G, a_in))
    return _from_blocks(o), S

def mlstm_chunkwise(q, k, v, i_pre, f_pre, c0, n0, m0):
    dk = q.shape[-1]
    c = _chunk_len(q.shape[1])
    q = _to_blocks(q, c)
    k = _to_blocks(k, c) * (dk ** -0.5)
    v = _to_blocks(v, c)
    ig = _to_blocks(i_pre, c)
    b = jnp.cumsum(jax.nn.log_sigmoid(_to_blocks(f_pre, c)), axis=-1)
    incl = jnp.tril(jnp.ones((c, c), dtype=bool))
    dlog = jnp.where(incl, b[..., :, None] - b[..., None, :] + ig[..., None, :], -jnp.inf)

    def step(carry, xs):
        cs, ns, ms = carry
        qc, kc, vc, bc, ic, dc = xs
        inter = bc + ms[..., None]
        mt = jnp.maximum(inter, jnp.max(dc, axis=-1))
        w_inter = jnp.exp(inter - mt)
        s = jnp.einsum('bhik,bhjk->bhij', qc, kc) * jnp.exp(dc - mt[..., None])
        num = (w_inter[..., None] * jnp.einsum('bhck,bhkv->bhcv', qc, cs)
               + jnp.einsum('bhij,bhjv->bhiv', s, vc))
        den = w_inter * jnp.einsum('bhck,bhk->bhc', qc, ns) + jnp.sum(s, axis=-1)
        h = num / jnp.maximum(jnp.abs(den), jnp.exp(-mt))[..., None]
        m_end = mt[..., -1]
        a_end = jnp.exp(bc[..., -1] + ms - m_end)
        wk = jnp.exp(bc[..., -1:] - bc + ic - m_end[..., None])
        cs = a_end[..., None, None] * cs + jnp.einsum('bhck,bhcv->bhkv', kc * wk[..., None], vc)
        ns = a_end[..., None] * ns + jnp.einsum('bhck,bhc->bhk', kc, wk)
        return (cs, ns, m_end), h

    f32 = jnp.float32
    (cs, ns, ms), h = lax.scan(step, (c0.astype(f32), n0.astype(f32), m0.astype(f32)),
                               (q, k, v, b, ig, dlog))
    return _from_blocks(h), cs, ns, ms

def s5_ssm(u, h0_re, h0_im, lam_re, lam_im, log_dt, b_re, b_im, c_re, c_im, d):
    f32 = jnp.float32
    bsz, L, _ = u.shape
    ug = u.astype(f32).reshape(bsz, L, S5_GROUPS, S5_GROUP)
    lr, li = lam_re.astype(f32), lam_im.astype(f32)
    dt = jnp.exp(log_dt.astype(f32))[:, None]
    mag = jnp.exp(lr * dt)
    ar, ai = mag * jnp.cos(li * dt), mag * jnp.sin(li * dt)
    inv = 1.0 / (lr * lr + li * li)
    cr = ((ar - 1.0) * lr + ai * li) * inv
    ci = (ai * lr - (ar - 1.0) * li) * inv
    bur = jnp.einsum('blgc,gpc->blgp', ug, b_re.astype(f32))
    bui = jnp.einsum('blgc,gpc->blgp', ug, b_im.astype(f32))
    xr = cr * bur - ci * bui
    xi = cr * bui + ci * bur
    h0r, h0i = h0_re.astype(f32), h0_im.astype(f32)
    xr = xr.at[:, 0].add(ar * h0r - ai * h0i)
    xi = xi.at[:, 0].add(ar * h0i + ai * h0r)

    def combine(e1, e2):
        a1r, a1i, b1r, b1i = e1
        a2r, a2i, b2r, b2i = e2
        return (a2r * a1r - a2i * a1i, a2r * a1i + a2i * a1r,
                a2r * b1r - a2i * b1i + b2r, a2r * b1i + a2i * b1r + b2i)

    _, _, hr, hi = lax.associative_scan(
        combine, (jnp.broadcast_to(ar, xr.shape), jnp.broadcast_to(ai, xr.shape), xr, xi), axis=1)
    y = (jnp.einsum('blgp,gcp->blgc', hr, c_re.astype(f32))
         - jnp.einsum('blgp,gcp->blgc', hi, c_im.astype(f32))
         + d.astype(f32) * ug)
    return y.reshape(bsz, L, S5_WIDTH), hr[:, -1], hi[:, -1]

def cross_attn(h, mem_k, mem_v, wq, wo):
    b, L, _ = h.shape
    q = (h @ wq).reshape(b, L, X_HEADS, X_HD)
    s = jnp.einsum('blhd,bmhd->bhlm', q, mem_k).astype(jnp.float32) * (X_HD ** -0.5)
    p = jax.nn.softmax(s, axis=-1).astype(h.dtype)
    o = jnp.einsum('bhlm,bmhd->blhd', p, mem_v).reshape(b, L, X_WIDTH)
    return o @ wo

def decoder_layer(x, mem_k, mem_v, conv_buf, dn_s, ml_c, ml_n, ml_m, ssm_re, ssm_im, p):
    f32 = jnp.float32
    b, L, _ = x.shape
    h = rmsnorm(x, p['norm_mix'])
    z = h @ p['w_in']
    (d_q, d_k, d_v, d_beta, d_alpha, d_gate,
     l_q, l_k, l_v, l_i, l_f, l_o, s_u) = jnp.split(z, _split_points(), axis=-1)

    qkv, new_conv = causal_conv_silu(jnp.concatenate([d_q, d_k, d_v], axis=-1), conv_buf, p['dn_conv_w'])
    cq, ck, cv = jnp.split(qkv, [DN_QK, 2 * DN_QK], axis=-1)
    q = _l2norm(cq.reshape(b, L, DN_HEADS, DN_DK))
    k = _l2norm(ck.reshape(b, L, DN_HEADS, DN_DK))
    v = cv.reshape(b, L, DN_HEADS, DN_DV)
    beta = jax.nn.sigmoid(d_beta.astype(f32))
    g = -jnp.exp(p['dn_a_log'].astype(f32)) * jax.nn.softplus(d_alpha.astype(f32) + p['dn_dt_bias'].astype(f32))
    o, new_s = gated_delta_rule(q, k, v, g, beta, dn_s)
    o = rmsnorm(o, p['dn_norm']) * jax.nn.silu(d_gate.astype(f32).reshape(b, L, DN_HEADS, DN_DV))
    dn_out = o.reshape(b, L, DN_WIDTH)

    hm, new_c, new_n, new_m = mlstm_chunkwise(
        l_q.reshape(b, L, ML_HEADS, ML_DK), l_k.reshape(b, L, ML_HEADS, ML_DK),
        l_v.reshape(b, L, ML_HEADS, ML_DV),
        l_i.astype(f32) + p['ml_i_bias'].astype(f32), l_f.astype(f32) + p['ml_f_bias'].astype(f32),
        ml_c, ml_n, ml_m)
    hm = rmsnorm(hm, p['ml_norm']) * jax.nn.sigmoid(l_o.astype(f32).reshape(b, L, ML_HEADS, ML_DV))
    ml_out = hm.reshape(b, L, ML_WIDTH)

    ys, new_re, new_im = s5_ssm(s_u, ssm_re, ssm_im, p['s5_lam_re'], p['s5_lam_im'], p['s5_log_dt'],
                                p['s5_b_re'], p['s5_b_im'], p['s5_c_re'], p['s5_c_im'], p['s5_d'])
    zg = jax.nn.gelu(ys)
    s5_out = zg * jax.nn.sigmoid(zg @ p['s5_w_glu'].astype(f32) + p['s5_b_glu'].astype(f32))

    mix = jnp.concatenate([dn_out, ml_out, s5_out], axis=-1).astype(x.dtype)
    x = x + mix @ p['w_out']
    x = x + cross_attn(rmsnorm(x, p['norm_x']), mem_k, mem_v, p['w_xq'], p['w_xo'])
    hf = rmsnorm(x, p['norm_ff']) @ p['w_ff1']
    x = x + jnp.square(jax.nn.relu(hf)) @ p['w_ff2']
    sd = x.dtype
    return x, (new_conv.astype(sd), new_s.astype(sd), new_c.astype(sd), new_n.astype(sd),
               new_m.astype(sd), new_re.astype(sd), new_im.astype(sd))

def setup_inputs(seed: int = 0) -> dict:
    key = jax.random.key(seed)
    ks = iter(jax.random.split(key, 64))
    f32 = jnp.float32

    def nrm(shape, scale=1.0):
        return jax.random.normal(next(ks), shape, f32) * scale

    def unif(shape, lo, hi):
        return jax.random.uniform(next(ks), shape, f32, lo, hi)

    def gain(shape):
        return 1.0 + nrm(shape, 0.02)

    Dp = DEPTH
    dt0 = jnp.exp(unif((Dp, DN_HEADS), math.log(1e-3), math.log(1e-1)))
    inp = {}
    inp['x_prompt'] = nrm((BATCH, SEQ, D_MODEL))
    inp['x_sample'] = nrm((DEC_BATCH, DEC_SEQ, D_MODEL))
    inp['mem_prompt'] = nrm((BATCH, N_MEM, D_MODEL))
    inp['state_dn_conv'] = nrm((Dp, DEC_BATCH, CONV_W - 1, CONV_CH))
    inp['state_dn_s'] = nrm((Dp, DEC_BATCH, DN_HEADS, DN_DK, DN_DV), 0.3)
    inp['state_ml_c'] = nrm((Dp, DEC_BATCH, ML_HEADS, ML_DK, ML_DV), 0.3)
    inp['state_ml_n'] = nrm((Dp, DEC_BATCH, ML_HEADS, ML_DK), 0.3)
    inp['state_ml_m'] = nrm((Dp, DEC_BATCH, ML_HEADS))
    inp['state_ssm_re'] = nrm((Dp, DEC_BATCH, S5_GROUPS, S5_P), 0.5)
    inp['state_ssm_im'] = nrm((Dp, DEC_BATCH, S5_GROUPS, S5_P), 0.5)
    inp['cache_mem_k'] = nrm((Dp, DEC_BATCH, N_MEM, X_HEADS, X_HD))
    inp['cache_mem_v'] = nrm((Dp, DEC_BATCH, N_MEM, X_HEADS, X_HD))
    inp['norm_mix'] = gain((Dp, D_MODEL))
    inp['w_in'] = nrm((Dp, D_MODEL, P_IN), D_MODEL ** -0.5)
    inp['dn_conv_w'] = nrm((Dp, CONV_W, CONV_CH), 0.5)
    inp['dn_a_log'] = jnp.log(unif((Dp, DN_HEADS), 1.0, 16.0))
    inp['dn_dt_bias'] = dt0 + jnp.log(-jnp.expm1(-dt0))
    inp['dn_norm'] = gain((Dp, DN_DV))
    inp['ml_i_bias'] = nrm((Dp, ML_HEADS), 0.1)
    inp['ml_f_bias'] = unif((Dp, ML_HEADS), 3.0, 6.0)
    inp['ml_norm'] = gain((Dp, ML_DV))
    inp['s5_lam_re'] = -0.5 + nrm((Dp, S5_GROUPS, S5_P), 0.01)
    inp['s5_lam_im'] = (math.pi * jnp.arange(S5_P, dtype=f32))[None, None, :] + nrm((Dp, S5_GROUPS, S5_P), 0.01)
    inp['s5_log_dt'] = unif((Dp, S5_GROUPS), math.log(1e-3), math.log(1e-1))
    inp['s5_b_re'] = nrm((Dp, S5_GROUPS, S5_P, S5_GROUP), (2 * S5_GROUP) ** -0.5)
    inp['s5_b_im'] = nrm((Dp, S5_GROUPS, S5_P, S5_GROUP), (2 * S5_GROUP) ** -0.5)
    inp['s5_c_re'] = nrm((Dp, S5_GROUPS, S5_GROUP, S5_P), S5_P ** -0.5)
    inp['s5_c_im'] = nrm((Dp, S5_GROUPS, S5_GROUP, S5_P), S5_P ** -0.5)
    inp['s5_d'] = nrm((Dp, S5_GROUPS, S5_GROUP), 0.5)
    inp['s5_w_glu'] = nrm((Dp, S5_WIDTH, S5_WIDTH), S5_WIDTH ** -0.5)
    inp['s5_b_glu'] = nrm((Dp, S5_WIDTH), 0.02)
    inp['w_out'] = nrm((Dp, D_MODEL, D_MODEL), D_MODEL ** -0.5)
    inp['norm_x'] = gain((Dp, D_MODEL))
    inp['norm_mem'] = gain((Dp, D_MODEL))
    inp['w_xq'] = nrm((Dp, D_MODEL, X_WIDTH), D_MODEL ** -0.5)
    inp['w_xk'] = nrm((Dp, D_MODEL, X_WIDTH), D_MODEL ** -0.5)
    inp['w_xv'] = nrm((Dp, D_MODEL, X_WIDTH), D_MODEL ** -0.5)
    inp['w_xo'] = nrm((Dp, X_WIDTH, D_MODEL), X_WIDTH ** -0.5)
    inp['norm_ff'] = gain((Dp, D_MODEL))
    inp['w_ff1'] = nrm((Dp, D_MODEL, D_FF), D_MODEL ** -0.5)
    inp['w_ff2'] = nrm((Dp, D_FF, D_MODEL), D_FF ** -0.5)
    inp['norm_final'] = gain((D_MODEL,))
    return inp

def reference(x_prompt, x_sample, mem_prompt, state_dn_conv, state_dn_s, state_ml_c, state_ml_n,
              state_ml_m, state_ssm_re, state_ssm_im, cache_mem_k, cache_mem_v,
              norm_mix, w_in, dn_conv_w, dn_a_log, dn_dt_bias, dn_norm, ml_i_bias, ml_f_bias, ml_norm,
              s5_lam_re, s5_lam_im, s5_log_dt, s5_b_re, s5_b_im, s5_c_re, s5_c_im, s5_d, s5_w_glu, s5_b_glu,
              w_out, norm_x, norm_mem, w_xq, w_xk, w_xv, w_xo, norm_ff, w_ff1, w_ff2, norm_final):
    f32 = jnp.float32
    layers = [dict(norm_mix=norm_mix[l], w_in=w_in[l], dn_conv_w=dn_conv_w[l], dn_a_log=dn_a_log[l],
                   dn_dt_bias=dn_dt_bias[l], dn_norm=dn_norm[l], ml_i_bias=ml_i_bias[l],
                   ml_f_bias=ml_f_bias[l], ml_norm=ml_norm[l], s5_lam_re=s5_lam_re[l],
                   s5_lam_im=s5_lam_im[l], s5_log_dt=s5_log_dt[l], s5_b_re=s5_b_re[l], s5_b_im=s5_b_im[l],
                   s5_c_re=s5_c_re[l], s5_c_im=s5_c_im[l], s5_d=s5_d[l], s5_w_glu=s5_w_glu[l],
                   s5_b_glu=s5_b_glu[l], w_out=w_out[l], norm_x=norm_x[l], w_xq=w_xq[l], w_xo=w_xo[l],
                   norm_ff=norm_ff[l], w_ff1=w_ff1[l], w_ff2=w_ff2[l])
              for l in range(DEPTH)]

    bp = x_prompt.shape[0]
    sd = x_prompt.dtype
    z_conv = jnp.zeros((bp, CONV_W - 1, CONV_CH), sd)
    z_dn = jnp.zeros((bp, DN_HEADS, DN_DK, DN_DV), f32)
    z_mc = jnp.zeros((bp, ML_HEADS, ML_DK, ML_DV), f32)
    z_mn = jnp.zeros((bp, ML_HEADS, ML_DK), f32)
    z_mm = jnp.zeros((bp, ML_HEADS), f32)
    z_s = jnp.zeros((bp, S5_GROUPS, S5_P), f32)
    xp = x_prompt
    p_st = []
    for l in range(DEPTH):
        mn = rmsnorm(mem_prompt, norm_mem[l])
        mk = (mn @ w_xk[l]).reshape(bp, N_MEM, X_HEADS, X_HD)
        mv = (mn @ w_xv[l]).reshape(bp, N_MEM, X_HEADS, X_HD)
        xp, st = decoder_layer(xp, mk, mv, z_conv, z_dn, z_mc, z_mn, z_mm, z_s, z_s, layers[l])
        p_st.append(st + (mk, mv))
    y_prompt = rmsnorm(xp, norm_final)

    xs = x_sample
    s_st = []
    for l in range(DEPTH):
        xs, st = decoder_layer(xs, cache_mem_k[l], cache_mem_v[l], state_dn_conv[l], state_dn_s[l],
                               state_ml_c[l], state_ml_n[l], state_ml_m[l], state_ssm_re[l],
                               state_ssm_im[l], layers[l])
        s_st.append(st)
    y_sample = rmsnorm(xs, norm_final)

    p_dn_conv = jnp.stack([s[0] for s in p_st])
    p_dn_s = jnp.stack([s[1] for s in p_st])
    p_ml_c = jnp.stack([s[2] for s in p_st])
    p_ml_n = jnp.stack([s[3] for s in p_st])
    p_ml_m = jnp.stack([s[4] for s in p_st])
    p_ssm_re = jnp.stack([s[5] for s in p_st])
    p_ssm_im = jnp.stack([s[6] for s in p_st])
    p_mem_k = jnp.stack([s[7] for s in p_st])
    p_mem_v = jnp.stack([s[8] for s in p_st])
    s_dn_conv = jnp.stack([s[0] for s in s_st])
    s_dn_s = jnp.stack([s[1] for s in s_st])
    s_ml_c = jnp.stack([s[2] for s in s_st])
    s_ml_n = jnp.stack([s[3] for s in s_st])
    s_ml_m = jnp.stack([s[4] for s in s_st])
    s_ssm_re = jnp.stack([s[5] for s in s_st])
    s_ssm_im = jnp.stack([s[6] for s in s_st])
    return (y_prompt, y_sample, p_dn_conv, p_dn_s, p_ml_c, p_ml_n, p_ml_m, p_ssm_re, p_ssm_im,
            p_mem_k, p_mem_v, s_dn_conv, s_dn_s, s_ml_c, s_ml_n, s_ml_m, s_ssm_re, s_ssm_im)


_drawn_inputs = setup_inputs


def setup_inputs(seed=0):
    import zlib

    import numpy as np

    out = dict(_drawn_inputs(seed))
    spreads = {}
    factors = {'dn_norm': 8.0,
     'ml_norm': 8.0,
     's5_lam_re': 15.977,
     's5_b_glu': 64.0,
     'norm_x': 8.0,
     'norm_mem': 2.841,
     'norm_ff': 3.356,
     'norm_final': 8.415,
     's5_w_glu': 5.152}
    for name, (base, spread) in spreads.items():
        noise = np.random.default_rng([zlib.crc32(name.encode()), seed]).standard_normal(out[name].shape)
        drawn = base * np.exp(spread * noise) if base else spread * noise
        out[name] = jnp.asarray(drawn.astype(out[name].dtype))
    for name, factor in factors.items():
        out[name] = (out[name] * factor).astype(out[name].dtype)
    return out
```

```python
from contextlib import ExitStack

import numpy as np

import concourse.bass as bass
from concourse import mybir

F32 = mybir.dt.float32
ALU = mybir.AluOpType
ACT = mybir.ActivationFunctionType
AX = mybir.AxisListType

P = 128
D = 1024
KT = D // P
SEQ, DB, DS = 1024, 8, 4
T = SEQ + DB * DS
NB, BW = 3, T // 3
PB2 = SEQ - 2 * BW
H, HD, NP = 6, 64, 3
CW = 64
NC = SEQ // CW
NMEM, XH, XD = 256, 4, 128
FF = 4096
FT = FF // P
CONV = 9
EXT = SEQ + 3 + DB * (DS + 3)
CO = EXT - 3
ST = 8
SB = DS + 1
TAU = SEQ + 1
LO = 9
EPS = 1e-6
BIG = 1e30
TWO_PI_HI = 6.28125
TWO_PI_MID = 0.0019350051879882812
TWO_PI_LO = 3.0198e-07
ROUND = 12582912.0
HALF_PI = 1.5707963705062866
PI = 3.1415925

PC = {}
_n = 0
for _name, _w in (("mix", KT), ("x", KT), ("ff", KT), ("final", KT), ("mem", KT), ("conv", CONV * 4),
                  ("dn", 1), ("ml", 1), ("dsel", ST), ("glu", 2), ("lr", ST), ("li", ST), ("ldt", ST),
                  ("bias", 1), ("alog", 1), ("m0", DB), ("eps", 1), ("eps64", 1), ("halfpi", 1), ("one", 1)):
    PC[_name] = _n
    _n += _w
NPC = _n
CC = {}
_n = 0
for _name, _w in (("ident", 128), ("ones", 128), ("heads", 128), ("rowsel", 5 * 3 * 128), ("colsel", 2 * 2 * 9),
                  ("causal", 3 * 64), ("off", 6 * 3 * 128), ("eye3", 3 * 128), ("blk3", 3 * 128)):
    CC[_name] = _n
    _n += _w
NCC = _n


class Steps:

    def __init__(self, eng, sem):
        self.eng, self.sem, self.n, self.reg, self.per = eng, sem, 0, None, 0

    def value(self):
        return self.n if self.reg is None else self.reg * self.per + self.n

    def __call__(self, ins, wait=True):
        ins.then_inc(self.sem, 1)
        self.n += 1
        if wait:
            self.eng.wait_ge(self.sem, self.value())

    def loop(self, reg, per, first=0):
        self.reg, self.per, self.start = reg, per, self.n
        self.n -= per * first

    def done(self, trips, first=0):
        assert self.n + self.per * first - self.start == self.per, (self.n + self.per * first - self.start, self.per)
        self.n = self.start + self.per * trips
        self.reg = None


def blk(b):
    return slice(b * BW, (b + 1) * BW)


def by_seq(ap, w=DS):
    return ap.rearrange("p (b t) -> p b t", t=w)


def alone(eng, n, passed, value):
    if not isinstance(n, int):
        eng.wait_ge(passed, value)


def is_first(n):
    return isinstance(n, int) and n == 0


def build(nc, t, o, upto=9):
    ctx = ExitStack()
    with ctx:
        place = {}

        def sb(name, shape):
            place[name] = nc.sbuf_base
            return ctx.enter_context(nc.sbuf_tensor(name, shape, F32))

        def rounded(name, shape):
            return nc.alloc_sbuf_tensor_at(name + "_r", shape, mybir.dt.float32r, offset=place[name])

        sems = {}

        def sem(name):
            if name not in sems:
                sems[name] = nc.alloc_semaphore(name=name)
            return sems[name]

        kept = ("h0_in", "braw_in", "c_in")

        def clear_semaphores():
            with nc.Block() as block:
                @block.sync
                def _(q):
                    for name, s in sems.items():
                        if name not in kept:
                            q.sem_clear(s)
            for name in [n for n in sems if n not in kept]:
                nc.release_semaphore(sems.pop(name))

        par = sb("par", [P, NPC])
        cst = sb("cst", [P, 3 * 128])
        feat = sb("feat", [P, 17 + CONV, T])
        u = feat[:, 0:2, :]
        zml = feat[:, 2:14, :]
        qkv = feat[:, 14:14 + CONV, :]
        zg = feat[:, 14 + CONV:17 + CONV, :]
        rows = sb("rows", [P, 2, T])
        regA = sb("regA", [P, KT * T])
        regH = sb("regH", [P, KT * T])
        regW = sb("regW", [P, 3 * KT * P])
        ext = sb("ext", [P, EXT])
        acc = sb("acc", [P, EXT])
        ps = [ctx.enter_context(nc.psum_tensor(f"ps{i}", [P, 512], F32)) for i in range(8)]
        ident, ones, heads = (cst[:, k * 128:(k + 1) * 128] for k in range(3))

        def pcol(name, k=0, n=1):
            return par[:, PC[name] + k:PC[name] + k + n]

        xv = regA[:, :].rearrange("p (k t) -> p k t", k=KT)
        hv = regH[:, :].rearrange("p (k t) -> p k t", k=KT)
        ring = [regW[:, s * KT * P:(s + 1) * KT * P] for s in range(3)]

        class Carve:
            def __init__(self, reg):
                self.reg, self.at = reg, 0

            def __call__(self, cols):
                self.at += cols
                assert self.at <= self.reg.shape[1], self.at
                return self.reg[:, self.at - cols:self.at]

        A = Carve(regA)
        F = A(2 * (TAU + DB * DS)).rearrange("p (c l) -> p c l", c=2)
        Fr, Fi = F[:, 0, :], F[:, 1, :]
        FL = A(2 * ST * LO).rearrange("p (c s l) -> p c s l", c=2, s=ST)
        G2 = A(2 * T)
        Gr, Gi = G2[:, 0:T], G2[:, T:2 * T]
        tt = A(2 * BW)
        t1, t2 = tt[:, 0:BW], tt[:, BW:2 * BW]
        hs = A(4 * BW)
        hr = [hs[:, 0:BW], hs[:, BW:2 * BW]]
        hn = [hs[:, 2 * BW:3 * BW], hs[:, 3 * BW:4 * BW]]
        pt = A(2 * BW)
        pt1, pt2 = pt[:, 0:BW], pt[:, BW:2 * BW]
        braw, bT, ctab = A(256), A(256), A(256)
        bsc = Gr[:, 600:856]
        sp = A(14 * ST).rearrange("p (n s) -> p n s", n=14)
        h0 = A(2 * ST * DB).rearrange("p (c s b) -> p c s b", c=2, s=ST)
        hend = A(2 * ST * (1 + DB)).rearrange("p (c s b) -> p c s b", c=2, s=ST)
        rdec = A(DB * DS)
        resets = sb("resets", [P, DB * DS])
        small = sb("small", [P, 16])
        M5 = sb("M5", [P, 3, DB * SB])
        cstate = sb("cstate", [P, CONV, 3 * DB])
        cnew = sb("cnew", [P, CONV, 3 + 3 * DB])
        mend = sb("mend", [P, 1 + DB])
        DT, LRD, TH, MAG, SIN, COS, KR, CR, CI, X1, X2, X3, X4, INV = range(14)

        for n in ("par_in cst_in x0 x1 x2 sq_ready sq_used sumsq_ready sumsq_ps root_ready h_ready w0 w1 w2 gemm evac "
                  "dve_step act_step pool_step braw_in c_in h0_in bsc_ready bT_ps bT_ready bu bu_used g_ready "
                  "pool_prod h_used hr_ready y_ps y_used s5_angle s5_trig ext_ready conv_in conv_ready silu_ready "
                  "sqr_ready l2_ps l2_root l2_done rows_in gates_raw r_act r_dve out_s").split():
            sem(n)
        GT = 2
        L1, L2 = 6, 2

        with nc.Block() as block:
            @block.sync
            def _(sp_):
                sp_.dma_start(par[:, :], t["par"]).then_inc(sem("par_in"), 16)
                sp_.dma_start(cst[:, :], t["cst"][:, 0:384]).then_inc(sem("cst_in"), 16)
                for b in range(NB):
                    sp_.dma_start(xv[:, :, blk(b)], t["xT"][:, :, blk(b)]).then_inc(sem(f"x{b}"), 16)
                for n in range(3):
                    sp_.dma_start(ring[n], t["w_in"][n]).then_inc(sem(f"w{n}"), 16)
                with sp_.Fori(0, L1) as i:
                    for k in range(3):
                        sp_.wait_ge(sem("gemm"), i * 9 + 3 * (k + 1))
                        sp_.dma_start(ring[k], t["w_in"][i * 3 + (3 + k)]).then_inc(sem(f"w{k}"), 16)
                with sp_.Fori(0, L2 + 1) as i:
                    for k in range(2):
                        sp_.wait_ge(sem("gemm"), i * 6 + 3 * (20 + k))
                        sp_.dma_start(ring[k], t["w_in"][i * 2 + (21 + k)]).then_inc(sem(f"w{k}"), 16)
                sp_.wait_ge(sem("hr_ready"), ST * NB)
                sp_.wait_ge(sem("hend_ready"), ST * 2)
                sp_.wait_ge(sem("pool_prod"), ST * NB * 2)
                sp_.dma_start(Fr[0:6, 0:SEQ], t["cmask"]).then_inc(sem("rows_in"), 16)
                sp_.dma_start(o["hend"], hend).then_inc(sem("out_s"), 16)
                sp_.wait_ge(sem("mend_ready"), 1)
                sp_.dma_start(o["mend"], mend[0:6, :]).then_inc(sem("out_s"), 16)
                sp_.wait_ge(sem("cnew_ready"), 1)
                sp_.dma_start(o["cnew"], cnew[:, :, :]).then_inc(sem("out_s"), 16)
                sp_.wait_ge(sem("out_s"), 48)

            @block.gpsimd
            def _(pool):
                pool.memset(ext[:, 0:3], 0.0).then_inc(sem("ext_ready"), 1)
                pool.dma_start(resets[:, :], t["resets"]).then_inc(sem("h0_in"), 16)
                pool.dma_start(cstate[:, :, :], t["cstate"]).then_inc(sem("h0_in"), 16)
                pool.wait_ge(sem("h_ready"), NB * KT)
                pool.dma_start(h0, t["h0"]).then_inc(sem("h0_in"), 16)

                def products(s):
                    if is_first(s):
                        pool.dma_start(braw, t["s5_b"][s]).then_inc(sem("braw_in"), 16)
                        pool.dma_start(ctab, t["s5_c"][:, s, :]).then_inc(sem("c_in"), 16)
                    else:
                        pool.wait_ge(sem("bsc_ready"), s)
                        alone(pool, s, sem("h_ready"), NB * KT)
                        pool.dma_start(braw, t["s5_b"][s]).then_inc(sem("braw_in"), 16)
                        pool.wait_ge(sem("y_ps"), s * NB)
                        pool.dma_start(ctab, t["s5_c"][:, s, :]).then_inc(sem("c_in"), 16)
                    pool.wait_ge(sem("g_ready"), s + 1)
                    for b in range(NB):
                        if not (is_first(s) and b == 0):
                            pool.wait_ge(sem("hr_ready"), s * NB + b)
                        f = Fi[:, 1 + b * BW:1 + (b + 1) * BW]
                        pool.tensor_tensor(pt1, f, Gi[:, blk(b)], ALU.mult).then_inc(sem("pool_prod"), 1)
                        pool.tensor_tensor(pt2, f, Gr[:, blk(b)], ALU.mult).then_inc(sem("pool_prod"), 1)

                products(0)
                with pool.Fori(1, ST) as s:
                    products(s)

            @block.tensor
            def _(pe):
                def gemm(n, slot, loads, b):
                    if b == 0:
                        pe.wait_ge(sem(f"w{slot}"), loads * 16)
                    if not is_first(n):
                        pe.wait_ge(sem("evac"), n * 3 + (b - 2))
                    for k in range(KT):
                        ins = pe.matmul(ps[b][:, 0:BW], ring[slot][:, k * P:(k + 1) * P], hv[:, k, blk(b)],
                                        start=(k == 0), stop=(k == KT - 1))
                    ins.then_inc(sem("gemm"), 1)

                pe.wait_ge(sem("cst_in"), 16)
                for b in range(NB):
                    pe.wait_ge(sem("sumsq_ready"), (b + 1) * KT)
                    pe.matmul(ps[5 + b][:, 0:BW], ones, acc[:, blk(b)], start=True, stop=True).then_inc(sem("sumsq_ps"), 1)
                for n in range(3):
                    for b in range(NB):
                        if n == 0:
                            pe.wait_ge(sem("h_ready"), (b + 1) * KT)
                        gemm(n, n, 1, b)

                def scaled_b(s):
                    pe.wait_ge(sem("bsc_ready"), s + 1)
                    if not is_first(s):
                        pe.wait_ge(sem("y_used"), s * NB)
                    pe.transpose(ps[5][:, 0:128], bsc[:, 0:128], ident)
                    pe.transpose(ps[5][:, 128:256], bsc[:, 128:256], ident).then_inc(sem("bT_ps"), 1)

                def s5_in(s, half, b):
                    if b == 0:
                        pe.wait_ge(sem("bT_ready"), s + 1)
                    if not (is_first(s) and b == 0):
                        pe.wait_ge(sem("bu_used"), s * NB + b)
                    pe.matmul(ps[3][:, 0:BW], bT[:, 0:128], u[:, half, blk(b)], start=True, stop=True)
                    pe.matmul(ps[4][:, 0:BW], bT[:, 128:256], u[:, half, blk(b)], start=True, stop=True)\
                      .then_inc(sem("bu"), 1)

                def s5_out(s, b):
                    pe.wait_ge(sem("hr_ready"), s * NB + (b + 1))
                    if b == 0:
                        pe.wait_ge(sem("c_in"), s * 16 + 16)
                        pe.wait_ge(sem("bT_ready"), s + 1)
                    if not (is_first(s) and b == 0):
                        pe.wait_ge(sem("y_used"), s * NB + b)
                    pe.matmul(ps[5][:, 0:BW], ctab[:, 0:128], hr[b % 2], start=True, stop=False)
                    pe.matmul(ps[5][:, 0:BW], ctab[:, 128:256], hn[b % 2], start=False, stop=True)\
                      .then_inc(sem("y_ps"), 1)

                def l2_sums(i):
                    pe.wait_ge(sem("sqr_ready"), i + 1)
                    for b in range(NB):
                        if b == 2 or not is_first(i):
                            pe.wait_ge(sem("l2_root"), i * NB + b // 2)
                        pe.matmul(ps[6 + b % 2][:, 0:BW], heads, ext[:, 3 + b * BW:3 + (b + 1) * BW],
                                  start=True, stop=True).then_inc(sem("l2_ps"), 1)

                def turn(n, loads, s, half, norm, third, i=0):
                    for b in range(NB):
                        gemm(n, 0, loads, b)
                        if not is_first(s):
                            s5_out(s - 1, b)
                    scaled_b(s)
                    gemm(n + 1, 1, loads, 0)
                    s5_in(s, half, 0)
                    gemm(n + 1, 1, loads, 1)
                    if norm:
                        l2_sums(i)
                    s5_in(s, half, 1)
                    gemm(n + 1, 1, loads, 2)
                    s5_in(s, half, 2)
                    if third:
                        for b in range(NB):
                            gemm(n + 2, 2, loads, b)

                turn(3, 2, 0, 0, True, True, 0)
                with pe.Fori(1, L1) as i:
                    turn(i * 3 + 3, i + 2, i, i // 4, True, True, i)
                with pe.Fori(0, L2) as i:
                    turn(i * 2 + 21, i + 8, i + 6, 1, False, False)
                for b in range(NB):
                    gemm(25, 0, 10, b)
                    s5_out(ST - 1, b)
                for b in range(NB):
                    gemm(26, 1, 10, b)

            @block.scalar
            def _(act):
                step = Steps(act, sem("act_step"))
                act.wait_ge(sem("par_in"), 16)
                for b in range(NB):
                    act.wait_ge(sem(f"x{b}"), 16)
                    for k in range(KT):
                        n = b * KT + k
                        if n >= 2:
                            act.wait_ge(sem("sumsq_ready"), n - 1)
                        act.activation(ext[:, 3 + (n % 2) * BW:3 + (n % 2 + 1) * BW], xv[:, k, blk(b)], ACT.Square)\
                           .then_inc(sem("sq_ready"), 1)
                for b in range(NB):
                    act.wait_ge(sem("sumsq_ps"), b + 1)
                    act.activation(qkv[:, 1, blk(b)], ps[5 + b][:, 0:BW], ACT.Sqrt, bias=pcol("eps"), scale=1.0 / D)\
                       .then_inc(sem("root_ready"), 1)

                def evac(n, b, dst):
                    act.wait_ge(sem("gemm"), n * 3 + (b + 1))
                    alone(act, n, sem("par_in"), 16)
                    act.activation(dst, ps[b][:, 0:BW], ACT.Copy).then_inc(sem("evac"), 1)

                for n in range(2):
                    for b in range(NB):
                        evac(n, b, u[:, n, blk(b)])
                act.activation(sp[:, DT, :], pcol("ldt", 0, ST), ACT.Exp).then_inc(sem("s5_trig"), 1)
                act.wait_ge(sem("s5_angle"), 1)
                act.activation(sp[:, MAG, :], sp[:, LRD, :], ACT.Exp).then_inc(sem("s5_trig"), 1)
                act.wait_ge(sem("s5_angle"), 2)
                act.activation(sp[:, SIN, :], sp[:, SIN, :], ACT.Sin).then_inc(sem("s5_trig"), 1)
                act.activation(sp[:, COS, :], sp[:, COS, :], ACT.Sin).then_inc(sem("s5_trig"), 1)
                for b in range(NB):
                    evac(GT, b, rows[:, 1, blk(b)])

                def evac_ext(j, n, b, last_norm):
                    act.wait_ge(sem("gemm"), n * 3 + (b + 1))
                    if b == 0:
                        if is_first(j):
                            act.wait_ge(sem("sumsq_ready"), NB * KT)
                        else:
                            act.wait_ge(sem("conv_ready"), j)
                            act.wait_ge(sem("l2_ps"), last_norm)
                    if b < 2:
                        act.activation(ext[:, 3 + b * BW:3 + (b + 1) * BW], ps[b][:, 0:BW], ACT.Copy)\
                           .then_inc(sem("evac"), 1)
                    else:
                        act.activation(ext[:, 3 + 2 * BW:3 + SEQ], ps[b][:, 0:PB2], ACT.Copy)\
                           .then_inc(sem("ext_ready"), 1)
                        act.activation(by_seq(ext[:, SEQ + 3:EXT], 7)[:, :, 3:7], by_seq(ps[b][:, PB2:BW]), ACT.Copy)\
                           .then_inc(sem("evac"), 1)

                def silu(j):
                    act.wait_ge(sem("conv_ready"), j + 1)
                    alone(act, j, sem("par_in"), 16)
                    act.activation(qkv[:, j, 0:SEQ], acc[:, 0:SEQ], ACT.Silu).then_inc(sem("silu_ready"), 1)
                    act.activation(by_seq(qkv[:, j, SEQ:T]), by_seq(acc[:, SEQ + 3:SEQ + 3 + DB * 7], 7)[:, :, 0:DS],
                                   ACT.Silu).then_inc(sem("silu_ready"), 1)

                def turned_b(s):
                    act.wait_ge(sem("bT_ps"), s + 1)
                    if not is_first(s):
                        act.wait_ge(sem("bu"), s * NB)
                    act.activation(bT, ps[5][:, 0:256], ACT.Copy).then_inc(sem("bT_ready"), 1)

                def qk_turn(i, n, z):
                    for b in range(NB):
                        evac_ext(i, n, b, i * NB)
                    evac(n + 1, 0, zml[:, z, blk(0)])
                    silu(i)
                    act.wait_ge(sem("silu_ready"), i * 2 + 2)
                    turned_b(i)
                    act.activation(ext[:, 3:3 + T], qkv[:, i, :], ACT.Square).then_inc(sem("sqr_ready"), 1)
                    evac(n + 1, 1, zml[:, z, blk(1)])
                    for b in range(NB):
                        act.wait_ge(sem("l2_ps"), i * NB + (b + 1))
                        act.activation(acc[:, blk(b)], ps[6 + b % 2][:, 0:BW], ACT.Sqrt,
                                       bias=small[:, 0:1], scale=small[:, 1:2]).then_inc(sem("l2_root"), 1)
                    evac(n + 1, 2, zml[:, z, blk(2)])
                    for b in range(NB):
                        evac(n + 2, b, zml[:, z + 1, blk(b)])

                def v_turn(j, s, n, g):
                    for b in range(NB):
                        evac_ext(j, n, b, L1 * NB)
                    if s is not None:
                        turned_b(s)
                    evac(n + 1, 0, zg[:, g, blk(0)])
                    silu(j)
                    evac(n + 1, 1, zg[:, g, blk(1)])
                    evac(n + 1, 2, zg[:, g, blk(2)])

                qk_turn(0, 3, 0)
                with act.Fori(1, L1) as i:
                    qk_turn(i, i * 3 + 3, i * 2)
                with act.Fori(0, L2) as i:
                    v_turn(i + 6, i + 6, i * 2 + 21, i)
                v_turn(8, None, 25, 2)

                act.wait_ge(sem("y_ps"), ST * NB)
                raw, bias, one = rows[:, 1, :], pcol("bias"), pcol("one")[0:6]
                w1, w2, w3 = Gr[0:6, :], Gi[0:6, :], hs[0:6, 0:T]
                act.activation(small[0:6, 2:3], pcol("alog")[0:6], ACT.Exp).then_inc(sem("r_act"), 1)
                step(act.activation(w1, raw[32:38, :], ACT.Abs, bias=bias[32:38]))
                step(act.activation(w1, w1, ACT.Exp, scale=-1.0))
                act.activation(w1, w1, ACT.Ln, bias=one).then_inc(sem("r_act"), 1)
                act.activation(w2, raw[32:38, :], ACT.Relu, bias=bias[32:38]).then_inc(sem("r_act"), 1)
                act.activation(w3, raw[64:70, :], ACT.Identity, bias=bias[64:70]).then_inc(sem("r_act"), 1)
                act.wait_ge(sem("r_dve"), 1)
                act.activation(w1, raw[96:102, :], ACT.Identity, bias=bias[96:102]).then_inc(sem("r_act"), 1)
                step(act.activation(w2, raw[96:102, :], ACT.Abs, bias=bias[96:102]))
                step(act.activation(w2, w2, ACT.Exp, scale=-1.0))
                act.activation(w2, w2, ACT.Ln, bias=one).then_inc(sem("r_act"), 1)
                act.activation(rows[32:38, 0, :], raw[0:6, :], ACT.Sigmoid).then_inc(sem("r_act"), 1)

            @block.vector
            def _(dve):
                step = Steps(dve, sem("dve_step"))
                for b in range(NB):
                    for k in range(KT):
                        n = b * KT + k
                        dve.wait_ge(sem("sq_ready"), n + 1)
                        sq = ext[:, 3 + (n % 2) * BW:3 + (n % 2 + 1) * BW]
                        if k == 0:
                            dve.tensor_copy(acc[:, blk(b)], sq).then_inc(sem("sumsq_ready"), 1)
                        else:
                            dve.tensor_tensor(acc[:, blk(b)], acc[:, blk(b)], sq, ALU.add).then_inc(sem("sumsq_ready"), 1)
                        dve.wait_ge(sem("sumsq_ready"), n + 1)
                for b in range(NB):
                    dve.wait_ge(sem("root_ready"), b + 1)
                    step(dve.reciprocal(qkv[:, 0, blk(b)], qkv[:, 1, blk(b)]))
                    for k in range(KT):
                        dve.scalar_tensor_tensor(hv[:, k, blk(b)], xv[:, k, blk(b)], pcol("mix", k), qkv[:, 0, blk(b)],
                                                 ALU.mult, ALU.mult).then_inc(sem("h_ready"), 1)
                dve.wait_ge(sem("h_ready"), NB * KT)

                lr, li = pcol("lr", 0, ST), pcol("li", 0, ST)

                def S(k):
                    return sp[:, k, :]

                def tt2(out, a, b, op):
                    step(dve.tensor_tensor(out, a, b, op))

                dve.wait_ge(sem("s5_trig"), 1)
                tt2(S(TH), li, S(DT), ALU.mult)
                dve.tensor_tensor(S(LRD), lr, S(DT), ALU.mult).then_inc(sem("s5_angle"), 1)
                step(dve.tensor_scalar(S(KR), S(TH), 0.15915494309189535, ROUND, ALU.mult, ALU.add))
                step(dve.tensor_scalar(S(KR), S(KR), ROUND, None, ALU.subtract))
                for part in (TWO_PI_HI, TWO_PI_MID, TWO_PI_LO):
                    step(dve.scalar_tensor_tensor(S(TH), S(KR), -part, S(TH), ALU.mult, ALU.add))
                step(dve.tensor_scalar(S(SIN), S(TH), PI, -PI, ALU.min, ALU.max))
                step(dve.scalar_tensor_tensor(S(COS), S(SIN), -1.0, S(SIN), ALU.mult, ALU.min))
                dve.tensor_scalar(S(COS), S(COS), HALF_PI, None, ALU.add).then_inc(sem("s5_angle"), 1)
                dve.wait_ge(sem("s5_trig"), 4)
                tt2(S(X1), S(MAG), S(COS), ALU.mult)
                tt2(S(X2), S(MAG), S(SIN), ALU.mult)
                step(dve.tensor_scalar(S(X1), S(X1), 1.0, None, ALU.subtract))
                tt2(S(X3), lr, lr, ALU.mult)
                tt2(S(X4), li, li, ALU.mult)
                tt2(S(X3), S(X3), S(X4), ALU.add)
                step(dve.reciprocal(S(INV), S(X3)))
                tt2(S(X3), S(X1), lr, ALU.mult)
                tt2(S(X4), S(X2), li, ALU.mult)
                tt2(S(X3), S(X3), S(X4), ALU.add)
                tt2(S(CR), S(X3), S(INV), ALU.mult)
                tt2(S(X3), S(X2), lr, ALU.mult)
                tt2(S(X4), S(X1), li, ALU.mult)
                tt2(S(X3), S(X3), S(X4), ALU.subtract)
                tt2(S(CI), S(X3), S(INV), ALU.mult)
                step(dve.memset(FL[:, 0, :, 0:1], 1.0))
                step(dve.memset(FL[:, 1, :, 0:1], 0.0))
                step(dve.tensor_copy(FL[:, 0, :, 1:2], S(COS).unsqueeze(2)))
                step(dve.tensor_copy(FL[:, 1, :, 1:2], S(SIN).unsqueeze(2)))
                for z in (1, 2, 4):
                    q1 = t1[:, 0:ST * z].rearrange("p (s l) -> p s l", s=ST)
                    q2 = t2[:, 0:ST * z].rearrange("p (s l) -> p s l", s=ST)
                    zr = FL[:, 0, :, z:z + 1].to_broadcast([P, ST, z])
                    zi = FL[:, 1, :, z:z + 1].to_broadcast([P, ST, z])
                    ar, ai = FL[:, 0, :, 1:z + 1], FL[:, 1, :, 1:z + 1]
                    tt2(q1, ar, zr, ALU.mult)
                    tt2(q2, ai, zi, ALU.mult)
                    tt2(FL[:, 0, :, z + 1:2 * z + 1], q1, q2, ALU.subtract)
                    tt2(q1, ar, zi, ALU.mult)
                    tt2(q2, ai, zr, ALU.mult)
                    tt2(FL[:, 1, :, z + 1:2 * z + 1], q1, q2, ALU.add)
                step(dve.memset(small[:, 0:1], 64.0 * EPS))
                step(dve.memset(small[:, 1:2], 64.0))

                def s5_tables(s):
                    cr, ci = sp[:, CR, s].unsqueeze(1), sp[:, CI, s].unsqueeze(1)
                    dve.wait_ge(sem("braw_in"), s * 16 + 16)
                    if not is_first(s):
                        dve.wait_ge(sem("pool_prod"), s * NB * 2)
                    br, bi = braw[:, 0:128], braw[:, 128:256]
                    step(dve.tensor_scalar(t1[:, 0:128], bi, ci, None, ALU.mult), wait=False)
                    step(dve.tensor_scalar(t2[:, 0:128], br, ci, None, ALU.mult))
                    step(dve.scalar_tensor_tensor(bsc[:, 0:128], br, cr, t1[:, 0:128], ALU.mult, ALU.subtract))
                    dve.scalar_tensor_tensor(bsc[:, 128:256], bi, cr, t2[:, 0:128], ALU.mult, ALU.add)\
                       .then_inc(sem("bsc_ready"), 1)
                    dve.wait_ge(sem("bsc_ready"), s + 1)
                    step(dve.tensor_copy(F[:, :, 0:LO], FL[:, :, s, :]))
                    z = LO - 1
                    while z < SEQ:
                        zr, zi = Fr[:, z:z + 1], Fi[:, z:z + 1]
                        step(dve.tensor_scalar(Gr[:, 0:z], Fi[:, 1:z + 1], zi, None, ALU.mult), wait=False)
                        step(dve.tensor_scalar(Gi[:, 0:z], Fr[:, 1:z + 1], zi, None, ALU.mult))
                        step(dve.scalar_tensor_tensor(Fr[:, z + 1:2 * z + 1], Fr[:, 1:z + 1], zr, Gr[:, 0:z],
                                                      ALU.mult, ALU.subtract), wait=False)
                        step(dve.scalar_tensor_tensor(Fi[:, z + 1:2 * z + 1], Fi[:, 1:z + 1], zr, Gi[:, 0:z],
                                                      ALU.mult, ALU.add))
                        z *= 2
                    for c in range(2):
                        step(dve.tensor_copy(by_seq(F[:, c, TAU:TAU + DB * DS]),
                                             F[:, c, 1:1 + DS].unsqueeze(1).to_broadcast([P, DB, DS])))

                def s5_rotate(s, b):
                    dve.wait_ge(sem("bu"), s * NB + (b + 1))
                    fr, fi = (F[:, c, 1 + b * BW:1 + (b + 1) * BW] for c in range(2))
                    xr, xi = ps[3][:, 0:BW], ps[4][:, 0:BW]
                    step(dve.tensor_tensor(t1, xr, fr, ALU.mult), wait=False)
                    step(dve.tensor_tensor(t2, xi, fi, ALU.mult))
                    step(dve.tensor_tensor(Gr[:, blk(b)], t1, t2, ALU.add))
                    step(dve.tensor_tensor(t1, xi, fr, ALU.mult), wait=False)
                    dve.tensor_tensor(t2, xr, fi, ALU.mult).then_inc(sem("bu_used"), 1)
                    dve.wait_ge(sem("bu_used"), s * NB + (b + 1))
                    step(dve.tensor_tensor(Gi[:, blk(b)], t1, t2, ALU.subtract))

                def s5_scan(s):
                    mag = sp[:, MAG, s].unsqueeze(1)
                    step(dve.tensor_scalar(rdec, resets[:, :], mag, None, ALU.mult), wait=False)
                    for c, g in ((0, Gr), (1, Gi)):
                        at0 = by_seq(g[:, SEQ:T])[:, :, 0:1]
                        step(dve.scalar_tensor_tensor(at0, h0[:, c, s, :].unsqueeze(2), mag, at0, ALU.mult, ALU.add))
                    for c, g in ((0, Gr), (1, Gi)):
                        step(dve.tensor_tensor_scan(g[:, 0:SEQ], mag.to_broadcast([P, SEQ]), g[:, 0:SEQ], 0.0,
                                                    ALU.mult, ALU.add))
                    step(dve.tensor_tensor_scan(Gr[:, SEQ:T], rdec, Gr[:, SEQ:T], 0.0, ALU.mult, ALU.add))
                    dve.tensor_tensor_scan(Gi[:, SEQ:T], rdec, Gi[:, SEQ:T], 0.0, ALU.mult, ALU.add)\
                       .then_inc(sem("g_ready"), 1)
                    dve.wait_ge(sem("g_ready"), s + 1)

                def s5_states(s):
                    for b in range(NB):
                        fr = Fr[:, 1 + b * BW:1 + (b + 1) * BW]
                        if b:
                            dve.wait_ge(sem("hr_ready"), s * NB + b)
                        step(dve.tensor_tensor(t1, fr, Gr[:, blk(b)], ALU.mult), wait=False)
                        step(dve.tensor_tensor(t2, fr, Gi[:, blk(b)], ALU.mult))
                        dve.wait_ge(sem("pool_prod"), s * NB * 2 + 2 * (b + 1))
                        if b == 2:
                            dve.wait_ge(sem("y_ps"), s * NB + 1)
                        step(dve.tensor_tensor(hr[b % 2], t1, pt1, ALU.subtract))
                        dve.scalar_tensor_tensor(hn[b % 2], t2, -1.0, pt2, ALU.mult, ALU.subtract)\
                           .then_inc(sem("hr_ready"), 1)
                    dve.wait_ge(sem("hr_ready"), s * NB + NB)
                    for c, h, f in ((0, hr[0], 1.0), (1, hn[0], -1.0)):
                        step(dve.tensor_scalar(hend[:, c, s, 0:1], h[:, PB2 - 1:PB2], f, None, ALU.mult), wait=False)
                        dve.tensor_scalar(hend[:, c, s, 1:1 + DB].unsqueeze(2), by_seq(h[:, PB2:BW])[:, :, DS - 1:DS],
                                          f, None, ALU.mult).then_inc(sem("hend_ready"), 1)

                def s5_outputs(s, half):
                    for b in range(NB):
                        dve.wait_ge(sem("y_ps"), s * NB + (b + 1))
                        dve.scalar_tensor_tensor(u[:, half, blk(b)], u[:, half, blk(b)], par[:, PC["dsel"]:PC["dsel"] + ST][:, s].unsqueeze(1),
                                                 ps[5][:, 0:BW], ALU.mult, ALU.add).then_inc(sem("y_used"), 1)

                def conv(j):
                    w = [par[:, PC["conv"]:PC["conv"] + CONV * 4].rearrange("p (j t) -> p j t", t=4)[:, j, k:k + 1]
                         for k in range(4)]
                    dve.wait_ge(sem("evac"), conv_at[0])
                    dve.wait_ge(sem("ext_ready"), j + 2)
                    if not is_first(j):
                        dve.wait_ge(sem("silu_ready"), j * 2)
                    sample = by_seq(ext[:, SEQ + 3:EXT], 7)
                    step(dve.tensor_copy(sample[:, :, 0:3], by_seq(cstate[:, j, :], 3)))
                    step(dve.tensor_copy(cnew[:, j, 0:3], ext[:, SEQ:SEQ + 3]), wait=False)
                    step(dve.tensor_copy(by_seq(cnew[:, j, 3:3 + 3 * DB], 3), sample[:, :, DS:DS + 3]), wait=False)
                    step(dve.tensor_scalar(acc[:, 0:CO], ext[:, 0:CO], w[0], None, ALU.mult))
                    for k in range(1, 4):
                        ins = dve.scalar_tensor_tensor(acc[:, 0:CO], ext[:, k:k + CO], w[k], acc[:, 0:CO], ALU.mult, ALU.add)
                        if k < 3:
                            step(ins)
                        else:
                            ins.then_inc(sem("conv_ready"), 1)

                conv_at = [None]

                def l2(i):
                    dve.wait_ge(sem("silu_ready"), i * 2 + 2)
                    for b in range(NB):
                        dve.wait_ge(sem("l2_root"), i * NB + (b + 1))
                        step(dve.reciprocal(acc[:, blk(b)], acc[:, blk(b)]))
                        step(dve.tensor_tensor(qkv[:, i, blk(b)], qkv[:, i, blk(b)], acc[:, blk(b)], ALU.mult))

                def turn(j, s, half, half_before, n, norm):
                    s5_tables(s)
                    if not is_first(s):
                        s5_outputs(s - 1, half_before)
                    conv_at[0] = n * 3 + 3
                    conv(j)
                    s5_rotate(s, 0)
                    if norm:
                        l2(j)
                    s5_rotate(s, 1)
                    s5_rotate(s, 2)
                    s5_scan(s)
                    s5_states(s)

                dve.wait_ge(sem("h0_in"), 48)
                before_turn = step.n
                turn(0, 0, 0, 0, 3, True)
                per = step.n - before_turn
                with dve.Fori(1, 3) as i:
                    step.loop(i, per, 1)
                    turn(i, i, 0, 0, i * 3 + 3, True)
                step.done(2, 1)
                step(dve.memset(small[:, 0:1], EPS))
                step(dve.memset(small[:, 1:2], 1.0))
                with dve.Fori(3, L1) as i:
                    step.loop(i, per, 3)
                    turn(i, i, i // 4, (i - 1) // 4, i * 3 + 3, True)
                step.done(3, 3)
                with dve.Fori(0, L2) as i:
                    step.loop(i, per - 2 * NB, 0)
                    turn(i + 6, i + 6, 1, 1, i * 2 + 21, False)
                step.done(2, 0)
                s5_outputs(ST - 1, 1)
                conv_at[0] = 25 * 3 + 3
                conv(8)
                dve.wait_ge(sem("dve_step"), step.n)
                dve.sem_inc(sem("cnew_ready"), 1)

                w1, w2, w3 = Gr[0:6, :], Gi[0:6, :], hs[0:6, 0:T]
                chunk0 = Fr[0:6, 0:SEQ]
                dve.wait_ge(sem("rows_in"), 16)
                dve.wait_ge(sem("r_act"), 3)
                step(dve.tensor_scalar(small[0:6, 3:4], small[0:6, 2:3], -1.0, None, ALU.mult))
                step(dve.tensor_tensor(w1, w1, w2, ALU.add))
                step(dve.tensor_scalar(w1, w1, small[0:6, 3:4], None, ALU.mult))
                step(dve.memset(rows[:, 0, :], 0.0))
                step(dve.tensor_tensor_scan(rows[0:6, 0, 0:SEQ], chunk0, w1[:, 0:SEQ], 0.0, ALU.mult, ALU.add))
                dve.tensor_tensor_scan(rows[0:6, 0, SEQ:T], resets[0:6, :], w1[:, SEQ:T], 0.0, ALU.mult, ALU.add)\
                   .then_inc(sem("r_dve"), 1)
                dve.wait_ge(sem("r_act"), 6)
                step(dve.scalar_tensor_tensor(w1, w1, 0.0, w2, ALU.min, ALU.subtract))
                step(dve.tensor_tensor_scan(w2[:, 0:SEQ], chunk0, w1[:, 0:SEQ], 0.0, ALU.mult, ALU.add))
                step(dve.tensor_tensor_scan(w2[:, SEQ:T], resets[0:6, :], w1[:, SEQ:T], 0.0, ALU.mult, ALU.add))
                m5 = [by_seq(M5[0:6, n, :], SB) for n in range(3)]
                step(dve.memset(M5[:, 0, :], -BIG))
                step(dve.tensor_copy(m5[0][:, :, 1:SB], by_seq(w1[:, SEQ:T])))
                step(dve.tensor_copy(m5[1][:, :, 1:SB], by_seq(w3[:, SEQ:T])))
                step(dve.tensor_copy(m5[1][:, :, 0:1], pcol("m0", 0, DB)[0:6].unsqueeze(2)))
                step(dve.tensor_tensor_scan(M5[0:6, 2, :], M5[0:6, 0, :], M5[0:6, 1, :], 0.0, ALU.add, ALU.max))
                dve.wait_ge(sem("r_act"), 7)
                step(dve.memset(rows[:, 1, :], 0.0))
                step(dve.tensor_copy(by_seq(rows[0:6, 1, SEQ:T]), m5[2][:, :, 1:SB]))
                step(dve.tensor_tensor_scan(rows[0:6, 1, 0:SEQ], w1[:, 0:SEQ], w3[:, 0:SEQ], 0.0, ALU.add, ALU.max))
                step(dve.tensor_tensor(w3, w3, w2, ALU.subtract))
                step(dve.tensor_scalar(rows[32:38, 1, :], w3, -2.0794415416798357, None, ALU.add))
                step(dve.tensor_tensor(w1, w2, rows[0:6, 1, :], ALU.subtract))
                step(dve.tensor_copy(rows[64:70, 0, :], w1))
                step(dve.tensor_copy(rows[96:102, 0, 0:CW], w1[:, 0:CW]))
                before = rows[0:6, 1, 0:SEQ].rearrange("p (c t) -> p c t", t=CW)[:, 0:NC - 1, CW - 1:CW]
                step(dve.tensor_tensor(w2[:, 0:SEQ - CW].rearrange("p (c t) -> p c t", t=CW),
                                       w1[:, CW:SEQ].rearrange("p (c t) -> p c t", t=CW),
                                       before.to_broadcast([6, NC - 1, CW]), ALU.add))
                step(dve.tensor_copy(rows[96:102, 0, CW:SEQ], w2[:, 0:SEQ - CW]))
                step(dve.tensor_tensor(by_seq(w2[:, SEQ:T]), by_seq(w1[:, SEQ:T]),
                                       m5[2][:, :, 0:1].to_broadcast([6, DB, DS]), ALU.add))
                step(dve.tensor_copy(rows[96:102, 0, SEQ:T], w2[:, SEQ:T]))
                step(dve.tensor_copy(mend[0:6, 0:1], rows[0:6, 1, SEQ - 1:SEQ]))
                dve.tensor_copy(mend[0:6, 1:1 + DB].unsqueeze(2), m5[2][:, :, DS:DS + 1]).then_inc(sem("mend_ready"), 1)
        if upto < 2:
            return
        clear_semaphores()

        A, B = Carve(regA), Carve(regH)

        def mats(carve):
            return carve(NP * P).rearrange("p (n m) -> p n m", n=NP)

        def thin(carve):
            return carve(NP * CW).rearrange("p (n m) -> p n m", n=NP)

        c2 = A(NCC - CC["rowsel"])

        def const(name, w):
            a = CC[name] - CC["rowsel"]
            return c2[:, a:a + w]

        rowsel = const("rowsel", 5 * 3 * P).rearrange("p (q n m) -> p q n m", q=5, n=3)
        colsel = const("colsel", 36).rearrange("p (h t c) -> p h t c", h=2, t=2)
        causal = const("causal", NP * CW).rearrange("p (n m) -> p n m", n=NP)
        off = const("off", 6 * NP * P).rearrange("p (l n m) -> p l n m", l=6, n=NP)
        eye3 = const("eye3", NP * P).rearrange("p (n m) -> p n m", n=NP)
        blk3 = const("blk3", NP * P).rearrange("p (n m) -> p n m", n=NP)

        kbd, vbd, mkbd, mvbd = (mats(B) for _ in range(4))
        Sol, Xb, Tb, MT, NCb, kdec, kbg, vb = ([mats(B) for v in range(2)] for _ in range(8))
        W2 = Carve(regW)
        st_dn, st_c, st_n = ([mats(W2) for v in range(2)] for _ in range(3))
        aT, qe, eG = ([thin(A) for v in range(2)] for _ in range(3))
        sT, qw, wI, emn = (thin(A) for _ in range(4))
        E1 = Carve(ext)
        tD, Dk, tM, tL, eL = (thin(E1) for _ in range(5))
        E2 = Carve(acc)
        kw, mvb = mats(E2), mats(E2)
        rs = E2(2 * CW).rearrange("p (n m) -> p n m", n=2)
        colS = E2(9)
        ein, eo, bg = E2(9), E2(9), E2(3)

        for n in ("c2_in zeroed bd_dn bd_ml rs gram bc_dn tok_dn cols_ready tD expD eG eo1 aT tM MT gram_used kv_used "
                  "nc0 nc1 Xp0 Xp1 X0 X1 Sp0 Sp1 S0 S1 Tp0 Tp1 T0 T1 wTp wT vp vn oTp dSp state_dn o_out bc_ml tok_ml "
                  "tL expL wI emn eo2 sT kw mvb qe qw nd cn num_out den_abs den_out state_ml ein1 ein2 dn_zero ml_zero b_step a_step "
                  "ld0 ld1 st_out").split():
            sem(n)
        PT, STN = NC // 2, DB // 2

        def wide(bank, k=0, w=CW):
            return bank[:, k * 192:(k + 1) * 192].rearrange("p (n m) -> p n m", n=NP)[:, :, 0:w]

        def full(bank):
            return bank[:, 0:NP * P].rearrange("p (n m) -> p n m", n=NP)

        def per_pair(col, w):
            return col.unsqueeze(2).to_broadcast([P, NP, w])

        class Chunk:

            def __init__(self, it, v, prompt):
                self.it, self.v, self.prompt = it, v, prompt
                self.c = it * 2 + v
                self.w = CW if prompt else DS
                self.levels = 6 if prompt else 2
                self.t0 = (it * 2 + v) * CW if prompt else (it * 2 + v) * DS + (SEQ - NC * DS)
                self.first = isinstance(it, int) and it == 0 and v == 0
                self.sv = 0 if prompt else v

            def tokens(self):
                return bass.ds(self.t0, self.w)

            def level(self, per, k):
                if self.prompt:
                    return self.it * per(6) + k
                return (self.it - PT) * per(2) + (PT * per(6) + k)

        PROMPT = ("fD", 0), ("fM", 0), ("S", 0), ("fD", 1), ("S", 1), ("L", 1), ("L", 2), ("rM", 0), ("L", 3), \
                 ("fM", 1), ("L", 4), ("L", 5), ("W", 0), ("W", 1), ("rD", 0), ("rM", 1), ("rD", 1)
        SAMPLE = ("fD", 0), ("fM", 0), ("S", 0), ("fD", 1), ("S", 1), ("L", 1), ("rM", 0), ("W", 0), ("W", 1), \
                 ("fM", 1), ("rD", 0), ("rM", 1), ("rD", 1)

        def go(eng, parts, between, step=None):
            def turn(it, prompt):
                ch = [Chunk(it, v, prompt) for v in range(2)]
                for name, k in (PROMPT if prompt else SAMPLE):
                    if name == "L":
                        parts[name](ch, k)
                    else:
                        parts[name](ch[k])

            n0 = step.n if step else 0
            turn(0, True)
            per = step.n - n0 if step else 0
            with eng.Fori(1, PT) as it:
                if step:
                    step.loop(it, per, 1)
                turn(it, True)
            if step:
                step.done(PT - 1, 1)
            between()
            with eng.Fori(PT, PT + STN) as it:
                if step:
                    step.loop(it, per, PT)
                turn(it, False)
            if step:
                step.done(STN, PT)

        with nc.Block() as block:
            @block.sync
            def _(q):
                q.dma_start(c2, t["cst"][:, CC["rowsel"]:NCC]).then_inc(sem("c2_in"), 16)

                def load(m, v):
                    for s, name in ((st_dn, "dn_s0"), (st_c, "ml_c0"), (st_n, "ml_n0")):
                        q.dma_start(s[v], t[name][m]).then_inc(sem(f"ld{v}"), 16)

                def store(k, v):
                    for s, name in ((st_dn, "dn_s"), (st_c, "ml_c"), (st_n, "ml_n")):
                        q.dma_start(o[name][k], s[v]).then_inc(sem("st_out"), 16)

                load(1, 1)
                q.wait_ge(sem("state_dn"), NC)
                q.wait_ge(sem("state_ml"), NC)
                store(0, 0)
                q.wait_ge(sem("st_out"), 48)
                load(0, 0)
                with q.Fori(0, STN - 1) as m:
                    for v in range(2):
                        q.wait_ge(sem("state_dn"), m * 2 + (NC + v + 1))
                        q.wait_ge(sem("state_ml"), m * 2 + (NC + v + 1))
                        store(m * 2 + (v + 1), v)
                        q.wait_ge(sem("st_out"), m * 96 + 48 * (v + 2))
                        load(m * 2 + (v + 2), v)
                for v in range(2):
                    q.wait_ge(sem("state_dn"), NC + DB - 1 + v)
                    q.wait_ge(sem("state_ml"), NC + DB - 1 + v)
                    store(DB - 1 + v, v)
                q.wait_ge(sem("st_out"), 48 * (1 + DB))

            @block.gpsimd
            def _(pool):
                for k, m in enumerate((kbd, vbd, mkbd, mvbd, MT[0], MT[1], NCb[0], NCb[1])):
                    pool.memset(m, 0.0).then_inc(sem("zeroed"), 1)
                pool.memset(colS, 0.0).then_inc(sem("zeroed"), 1)
                pool.wait_ge(sem("zeroed"), 9)
                pool.wait_ge(sem("c2_in"), 16)

                def halves(dst, src, ch, s, name, part):
                    for h in range(2):
                        r = slice(64 * h, 64 * h + 64)
                        pool.tensor_copy(dst[r, :, 64 * h:64 * h + ch.w], src[r, s:s + NP, ch.tokens()])\
                            .then_inc(sem(name), 1)
                        pool.wait_ge(sem(name), ch.c * 4 + (part + h + 1))

                def fD(ch):
                    if not ch.first:
                        pool.wait_ge(sem("tok_dn"), ch.c)
                        pool.wait_ge(sem("bc_dn"), ch.c)
                    halves(kbd, qkv, ch, 3, "bd_dn", 0)
                    halves(vbd, qkv, ch, 6, "bd_dn", 2)
                    pool.tensor_copy(rs[:, :, 0:ch.w], rows[:, :, ch.tokens()]).then_inc(sem("rs"), 1)
                    if not ch.first:
                        pool.wait_ge(sem("tok_ml"), ch.c)
                    halves(mkbd, zml, ch, 3, "bd_ml", 0)
                    halves(mvbd, zml, ch, 6, "bd_ml", 2)
                    pool.wait_ge(sem("eG"), ch.c + 1)
                    if not (ch.it == 0 if isinstance(ch.it, int) else False):
                        pool.wait_ge(sem("oTp"), ch.c - 1)
                    pool.tensor_tensor(qe[ch.v][:, :, 0:ch.w], qkv[:, 0:NP, ch.tokens()], eG[ch.v][:, :, 0:ch.w], ALU.mult)\
                        .then_inc(sem("qe"), 1)
                    pool.wait_ge(sem("MT"), ch.c + 1)
                    masked(ch, 1)

                def masked(ch, k):
                    v = ch.v
                    if not (k == 1 and isinstance(ch.it, int) and ch.it == 0):
                        pool.wait_ge(sem(f"Xp{v}"), ch.level(lambda n: n - 1, k - 1))
                    pool.tensor_tensor(NCb[v], MT[v], off[:, k], ALU.mult).then_inc(sem(f"nc{v}"), 1)

                def fM(ch):
                    pool.wait_ge(sem("wI"), ch.c + 1)
                    if not ch.first:
                        pool.wait_ge(sem("nd"), ch.c)
                    pool.tensor_tensor(qw[:, :, 0:ch.w], zml[:, 0:NP, ch.tokens()], wI[:, :, 0:ch.w], ALU.mult)\
                        .then_inc(sem("qw"), 1)

                def L(chs, k):
                    if k + 1 < chs[0].levels:
                        for ch in chs:
                            masked(ch, k + 1)

                def between():
                    pool.wait_ge(sem("tok_dn"), NC)
                    pool.wait_ge(sem("bc_dn"), NC)
                    pool.wait_ge(sem("tok_ml"), NC)
                    pool.wait_ge(sem("dSp"), NC)
                    pool.wait_ge(sem("bc_ml"), NC)
                    for m in (kbd, vbd, mkbd, mvbd, MT[0], MT[1]):
                        pool.memset(m, 0.0).then_inc(sem("zeroed"), 1)
                    pool.wait_ge(sem("zeroed"), 15)

                go(pool, {"S": lambda ch: None, "W": lambda ch: None, "fD": fD, "fM": fM, "L": L, "rM": lambda ch: None, "rD": lambda ch: None}, between)

            @block.tensor
            def _(pe):
                pe.wait_ge(sem("c2_in"), 16)
                pe.wait_ge(sem("zeroed"), 9)

                def triple(out, lhs, rhs, w=None, start=True, stop=True):
                    for p in range(NP):
                        ins = pe.matmul(out(p), lhs[:, p, :], rhs(p), start=start, stop=stop)
                    return ins

                def thin_out(bank, k, w):
                    return lambda p: bank[:, k * 192 + p * CW:k * 192 + p * CW + w]

                def wide_out(bank):
                    return lambda p: bank[:, p * P:(p + 1) * P]

                def mat(m):
                    return lambda p: m[:, p, :]

                def cols(src, s, ch):
                    return lambda p: src[:, s + p, ch.tokens()]

                def fD(ch):
                    c, w = ch.c, ch.w
                    pe.wait_ge(sem("bd_dn"), c * 4 + 4)
                    if not ch.first:
                        pe.wait_ge(sem("gram_used"), c)
                        pe.wait_ge(sem("o_out"), ch.it * 2)
                    triple(thin_out(ps[2], 0, w), kbd, cols(qkv, 3, ch))
                    triple(thin_out(ps[2], 1, w), kbd, cols(qkv, 0, ch)).then_inc(sem("gram"), 1)
                    pe.wait_ge(sem("rs"), c + 1)
                    if not ch.first:
                        pe.wait_ge(sem("MT"), c)
                        pe.wait_ge(sem("eG"), c)
                    for q in range(2):
                        for p in range(NP):
                            pe.matmul(thin_out(ps[3], q, w)(p), rowsel[:, q, p, :], rows[:, 0, ch.tokens()], start=True, stop=True)
                    for h in range(2):
                        for k in range(2):
                            ins = pe.matmul(ps[3][64 * h:64 * h + w, 384:393], rs[:, k, 0:w], colsel[:, h, k, :],
                                            start=(k == 0), stop=(k == 1))
                    ins.then_inc(sem("bc_dn"), 1)
                    if not ch.first:
                        pe.wait_ge(sem("kw"), c)
                        pe.wait_ge(sem("mvb"), c)
                        if not ch.v:
                            pe.wait_ge(sem("state_ml"), c)
                    for p in range(NP):
                        pe.transpose(wide_out(ps[6])(p), kbd[:, p, :], ident)
                    for p in range(NP):
                        ins = pe.transpose(wide_out(ps[7])(p), vbd[:, p, :], ident)
                    ins.then_inc(sem("tok_dn"), 1)

                def S0(ch):
                    turn_sol(ch, 0)

                def turn_sol(ch, k):
                    v = ch.v
                    pe.wait_ge(sem(f"S{v}"), ch.level(lambda n: n, k + 1))
                    for p in range(NP):
                        ins = pe.transpose(wide_out(ps[v])(p), Sol[v][:, p, :], ident)
                    ins.then_inc(sem(f"Tp{v}"), 1)

                def L(chs, k):
                    for ch in chs:
                        v = ch.v
                        pe.wait_ge(sem(f"nc{v}"), ch.level(lambda n: n - 1, k))
                        pe.wait_ge(sem(f"T{v}"), ch.level(lambda n: n - 1, k))
                        triple(wide_out(ps[v]), NCb[v], mat(Tb[v])).then_inc(sem(f"Xp{v}"), 1)
                    for ch in chs:
                        v = ch.v
                        pe.wait_ge(sem(f"X{v}"), ch.level(lambda n: n - 1, k))
                        triple(wide_out(ps[v]), Xb[v], mat(Sol[v])).then_inc(sem(f"Sp{v}"), 1)
                    if k + 1 < chs[0].levels:
                        for ch in chs:
                            turn_sol(ch, k)

                def fM(ch):
                    c, w = ch.c, ch.w
                    pe.wait_ge(sem("bd_ml"), c * 4 + 4)
                    if not ch.first:
                        pe.wait_ge(sem("den_abs"), c)
                        pe.wait_ge(sem("num_out"), c)
                        pe.wait_ge(sem("state_ml"), c)
                    for q in range(2):
                        for p in range(NP):
                            pe.matmul(thin_out(ps[4], q, w)(p), rowsel[:, 2 + q, p, :], rows[:, 0, ch.tokens()], start=True, stop=True)
                    for p in range(NP):
                        pe.matmul(thin_out(ps[5], 0, w)(p), rowsel[:, 4, p, :], rows[:, 1, ch.tokens()], start=True, stop=True)
                    triple(thin_out(ps[5], 1, w), mkbd, cols(zml, 0, ch)).then_inc(sem("bc_ml"), 1)
                    pe.wait_ge(sem("kv_used"), c + 1)
                    for p in range(NP):
                        pe.transpose(wide_out(ps[6])(p), mkbd[:, p, :], ident)
                    for p in range(NP):
                        ins = pe.transpose(wide_out(ps[7])(p), mvbd[:, p, :], ident)
                    ins.then_inc(sem("tok_ml"), 1)

                def rM(ch):
                    c, w = ch.c, ch.w
                    pe.wait_ge(sem("qw"), c + 1)
                    pe.wait_ge(sem("sT"), c + 1)
                    pe.wait_ge(sem("mvb"), c + 1)
                    pe.wait_ge(sem("kw"), c + 1)
                    pe.wait_ge(sem("emn"), c + 1)
                    if ch.v == 0:
                        pe.wait_ge(sem("kv_used"), c + 2)
                    if ch.prompt:
                        pe.wait_ge(sem("state_ml"), c + 0) if not ch.first else pe.wait_ge(sem("ml_zero"), 2)
                    else:
                        pe.wait_ge(sem(f"ld{ch.v}"), (ch.it - PT) * 48 + 48)
                    cs, ns = st_c[ch.sv], st_n[ch.sv]
                    for p in range(NP):
                        a = thin_out(ps[4], 0, w)(p)
                        pe.matmul(a, cs[:, p, :], qw[:, p, 0:w], start=True, stop=False)
                        pe.matmul(a, mvb[:, p, :], sT[:, p, 0:w], start=False, stop=True)
                    for p in range(NP):
                        a = thin_out(ps[4], 1, w)(p)
                        pe.matmul(a, ns[:, p, :], qw[:, p, 0:w], start=True, stop=False)
                        ins = pe.matmul(a, blk3[:, p, :], sT[:, p, 0:w], start=False, stop=True)
                    ins.then_inc(sem("nd"), 1)
                    triple(wide_out(ps[5]), kw, mat(mvb))
                    triple(wide_out(ps[6]), kw, mat(blk3)).then_inc(sem("cn"), 1)

                def W(ch):
                    v = ch.v
                    pe.wait_ge(sem(f"S{v}"), ch.level(lambda n: n, ch.levels))
                    triple(wide_out(ps[v]), kbg[v], mat(Sol[v])).then_inc(sem("wTp"), 1)

                def rD(ch):
                    c, w, v = ch.c, ch.w, ch.v
                    pe.wait_ge(sem("wT"), c + 1)
                    if ch.prompt:
                        pe.wait_ge(sem("state_dn"), c + 0) if not ch.first else pe.wait_ge(sem("dn_zero"), 1)
                    else:
                        pe.wait_ge(sem(f"ld{ch.v}"), (ch.it - PT) * 48 + 48)
                    sd = st_dn[ch.sv]
                    for p in range(NP):
                        a = wide_out(ps[v])(p)
                        pe.matmul(a, Sol[v][:, p, :], vb[v][:, p, :], start=True, stop=False)
                        ins = pe.matmul(a, Xb[v][:, p, :], sd[:, p, :], start=False, stop=True)
                    ins.then_inc(sem("vp"), 1)
                    pe.wait_ge(sem("vn"), c + 1)
                    triple(wide_out(ps[v]), kdec[v], mat(Tb[v])).then_inc(sem("dSp"), 1)
                    pe.wait_ge(sem("gram_used"), ch.it * 2 + 2)
                    pe.wait_ge(sem("qe"), c + 1)
                    if not ch.first:
                        pe.wait_ge(sem("o_out"), c)
                    for p in range(NP):
                        a = thin_out(ps[2], 0, w)(p)
                        pe.matmul(a, sd[:, p, :], qe[v][:, p, 0:w], start=True, stop=False)
                        ins = pe.matmul(a, Tb[v][:, p, :], aT[v][:, p, 0:w], start=False, stop=True)
                    ins.then_inc(sem("oTp"), 1)

                go(pe, {"S": S0, "W": W, "fD": fD, "fM": fM, "L": L, "rM": rM, "rD": rD}, lambda: None)

            @block.scalar
            def _(act):
                def fD(ch):
                    c, w, v = ch.c, ch.w, ch.v
                    act.wait_ge(sem("bc_dn"), c + 1)
                    if not (isinstance(ch.it, int) and ch.it == 0):
                        act.wait_ge(sem("state_dn"), c - 1)
                    act.activation(eG[v][:, :, 0:w], wide(ps[3], 0, w), ACT.Exp).then_inc(sem("eG"), 1)
                    act.wait_ge(sem("ein1"), c + 1)
                    act.activation(eo[:, 0:6], ein[:, 0:6], ACT.Exp).then_inc(sem("eo1"), 1)
                    act.wait_ge(sem("tD"), c + 1)
                    act.activation(Dk[:, :, 0:w], tD[:, :, 0:w], ACT.Exp).then_inc(sem("expD"), 1)

                def S0(ch):
                    copy_T(ch, 0)

                def copy_T(ch, k):
                    v = ch.v
                    act.wait_ge(sem(f"Tp{v}"), ch.level(lambda n: n - 1, k + 1))
                    act.activation(Tb[v], full(ps[v]), ACT.Copy).then_inc(sem(f"T{v}"), 1)

                def L(chs, k):
                    for ch in chs:
                        v = ch.v
                        act.wait_ge(sem(f"Xp{v}"), ch.level(lambda n: n - 1, k))
                        act.activation(Xb[v], full(ps[v]), ACT.Copy).then_inc(sem(f"X{v}"), 1)
                    if k + 1 < chs[0].levels:
                        for ch in chs:
                            copy_T(ch, k)

                def fM(ch):
                    c, w = ch.c, ch.w
                    act.wait_ge(sem("bc_ml"), c + 1)
                    if not ch.first:
                        act.wait_ge(sem("state_ml"), c)
                    act.activation(wI[:, :, 0:w], wide(ps[4], 1, w), ACT.Exp).then_inc(sem("wI"), 1)
                    if not ch.first:
                        act.wait_ge(sem("den_out"), c)
                    act.activation(emn[:, :, 0:w], wide(ps[5], 0, w), ACT.Exp, scale=-1.0).then_inc(sem("emn"), 1)
                    act.wait_ge(sem("ein2"), c + 1)
                    act.activation(eo[:, 6:9], ein[:, 6:9], ACT.Exp).then_inc(sem("eo2"), 1)
                    act.wait_ge(sem("tL"), c + 1)
                    act.activation(eL[:, :, 0:w], tL[:, :, 0:w], ACT.Exp).then_inc(sem("expL"), 1)
                    act.wait_ge(sem("tok_ml"), c + 1)
                    act.activation(mvb, full(ps[7]), ACT.Copy).then_inc(sem("mvb"), 1)

                def rM(ch):
                    c, w = ch.c, ch.w
                    act.wait_ge(sem("nd"), c + 1)
                    alone(act, c, sem("zeroed"), 9)
                    act.activation(zml[:, 3:6, ch.tokens()], wide(ps[4], 1, w), ACT.Abs).then_inc(sem("den_abs"), 1)
                    act.activation(zml[:, 0:3, ch.tokens()], wide(ps[4], 0, w), ACT.Copy).then_inc(sem("num_out"), 1)

                def W(ch):
                    act.wait_ge(sem("wTp"), ch.c + 1)
                    act.activation(Xb[ch.v], full(ps[ch.v]), ACT.Copy, scale=-1.0).then_inc(sem("wT"), 1)

                def rD(ch):
                    c, w, v = ch.c, ch.w, ch.v
                    act.wait_ge(sem("vp"), c + 1)
                    act.activation(Tb[v], full(ps[v]), ACT.Copy).then_inc(sem("vn"), 1)
                    act.wait_ge(sem("oTp"), c + 1)
                    alone(act, c, sem("zeroed"), 9)
                    act.activation(qkv[:, 0:3, ch.tokens()], wide(ps[2], 0, w), ACT.Copy).then_inc(sem("o_out"), 1)

                go(act, {"S": S0, "W": W, "fD": fD, "fM": fM, "L": L, "rM": rM, "rD": rD}, lambda: None)

            @block.vector
            def _(dve):
                step = Steps(dve, sem("b_step"))
                dve.memset(st_dn[0], 0.0).then_inc(sem("dn_zero"), 1)
                dve.memset(st_c[0], 0.0).then_inc(sem("ml_zero"), 1)
                dve.memset(st_n[0], 0.0).then_inc(sem("ml_zero"), 1)
                dve.wait_ge(sem("c2_in"), 16)
                dve.wait_ge(sem("zeroed"), 9)

                def fD(ch):
                    c, w, v = ch.c, ch.w, ch.v
                    dve.wait_ge(sem("eG"), c + 1)
                    for h in range(2):
                        step(dve.tensor_copy(colS[64 * h:64 * h + w, :], ps[3][64 * h:64 * h + w, 384:393]), wait=(h == 1))
                    g, beta = colS[:, 0:3], colS[:, 3:6]
                    if not ch.first:
                        dve.wait_ge(sem("eo2"), c)
                    step(dve.tensor_copy(ein[:, 0:3], g), wait=False)
                    dve.tensor_tensor(ein[:, 3:6].unsqueeze(2), wide(ps[3])[:, :, w - 1:w], g.unsqueeze(2), ALU.subtract)\
                        .then_inc(sem("ein1"), 1)
                    dve.wait_ge(sem("ein1"), c + 1)
                    step(dve.tensor_tensor(tD[:, :, 0:w], wide(ps[3], 0, w), per_pair(g, w), ALU.subtract))
                    dve.scalar_tensor_tensor(tD[:, :, 0:w], tD[:, :, 0:w], 0.0, causal[:, :, 0:w], ALU.min, ALU.add)\
                        .then_inc(sem("tD"), 1)
                    dve.wait_ge(sem("eo1"), c + 1)
                    step(dve.tensor_tensor(bg, beta, eo[:, 0:3], ALU.mult))
                    dve.wait_ge(sem("tok_dn"), c + 1)
                    if not (isinstance(ch.it, int) and ch.it == 0):
                        dve.wait_ge(sem("dSp"), c - 1)
                    step(dve.tensor_tensor(kbg[v], full(ps[6]), per_pair(bg, P), ALU.mult), wait=False)
                    step(dve.tensor_tensor(kdec[v], full(ps[6]), per_pair(eo[:, 3:6], P), ALU.mult), wait=False)
                    dve.tensor_tensor(vb[v], full(ps[7]), per_pair(beta, P), ALU.mult).then_inc(sem("kv_used"), 1)
                    dve.wait_ge(sem("expD"), c + 1)
                    dve.wait_ge(sem("gram"), c + 1)
                    step(dve.tensor_tensor(tM[:, :, 0:w], wide(ps[2], 0, w), Dk[:, :, 0:w], ALU.mult))
                    if not (isinstance(ch.it, int) and ch.it == 0):
                        dve.wait_ge(sem("oTp"), c - 1)
                    dve.tensor_tensor(aT[v][:, :, 0:w], wide(ps[2], 1, w), Dk[:, :, 0:w], ALU.mult).then_inc(sem("gram_used"), 1)
                    if not (isinstance(ch.it, int) and ch.it == 0):
                        dve.wait_ge(sem(f"nc{v}"), (ch.it * 5 if ch.prompt else (ch.it - PT) + 5 * PT))
                    for h in range(2):
                        r = slice(64 * h, 64 * h + 64)
                        ins = dve.tensor_tensor(MT[v][r, :, 64 * h:64 * h + w], tM[r, :, 0:w], wide(ps[3], 1, w)[r], ALU.mult)
                        if h == 0:
                            step(ins, wait=False)
                        else:
                            ins.then_inc(sem("MT"), 1)
                    dve.wait_ge(sem("b_step"), step.value())
                    dve.wait_ge(sem("MT"), c + 1)
                    step(dve.tensor_tensor(Sol[v], MT[v], off[:, 0], ALU.mult))
                    dve.tensor_tensor(Sol[v], Sol[v], eye3, ALU.add).then_inc(sem(f"S{v}"), 1)

                def L(chs, k):
                    for ch in chs:
                        v = ch.v
                        dve.wait_ge(sem(f"Sp{v}"), ch.level(lambda n: n - 1, k))
                        dve.tensor_tensor(Sol[v], full(ps[v]), Sol[v], ALU.add).then_inc(sem(f"S{v}"), 1)
                        dve.wait_ge(sem(f"S{v}"), ch.level(lambda n: n, k + 1))

                def fM(ch):
                    c, w = ch.c, ch.w
                    dve.wait_ge(sem("wI"), c + 1)
                    cj = colS[:, 6:9]
                    dve.tensor_tensor(ein[:, 6:9].unsqueeze(2), wide(ps[4])[:, :, w - 1:w], cj.unsqueeze(2), ALU.add)\
                        .then_inc(sem("ein2"), 1)
                    step(dve.tensor_tensor(tL[:, :, 0:w], wide(ps[4], 0, w), per_pair(cj, w), ALU.add))
                    dve.scalar_tensor_tensor(tL[:, :, 0:w], tL[:, :, 0:w], 0.0, causal[:, :, 0:w], ALU.min, ALU.add)\
                        .then_inc(sem("tL"), 1)
                    dve.wait_ge(sem("eo2"), c + 1)
                    dve.wait_ge(sem("tok_ml"), c + 1)
                    if not ch.first:
                        dve.wait_ge(sem("cn"), c)
                    dve.tensor_tensor(kw, full(ps[6]), per_pair(eo[:, 6:9], P), ALU.mult).then_inc(sem("kw"), 1)
                    dve.wait_ge(sem("expL"), c + 1)
                    dve.wait_ge(sem("emn"), c + 1)
                    if not ch.first:
                        dve.wait_ge(sem("nd"), c)
                    dve.tensor_tensor(sT[:, :, 0:w], wide(ps[5], 1, w), eL[:, :, 0:w], ALU.mult).then_inc(sem("sT"), 1)

                def rM(ch):
                    c, w = ch.c, ch.w
                    dve.wait_ge(sem("den_abs"), c + 1)
                    d = zml[:, 3:6, ch.tokens()]
                    dve.tensor_tensor(d, d, emn[:, :, 0:w], ALU.max).then_inc(sem("den_out"), 1)
                    dve.wait_ge(sem("cn"), c + 1)
                    for s, bank in ((st_c[ch.sv], ps[5]), (st_n[ch.sv], ps[6])):
                        for p in range(NP):
                            ins = dve.scalar_tensor_tensor(s[:, p, :], s[:, p, :], wI[:, p, w - 1:w], bank[:, p * P:(p + 1) * P],
                                                           ALU.mult, ALU.add)
                            if s is st_n[ch.sv] and p == NP - 1:
                                ins.then_inc(sem("state_ml"), 1)
                            else:
                                step(ins, wait=False)
                    dve.wait_ge(sem("b_step"), step.value())
                    dve.wait_ge(sem("state_ml"), c + 1)

                def rD(ch):
                    c, w, v = ch.c, ch.w, ch.v
                    dve.wait_ge(sem("oTp"), c + 1)
                    s = st_dn[ch.sv]
                    for p in range(NP):
                        ins = dve.scalar_tensor_tensor(s[:, p, :], s[:, p, :], eG[v][:, p, w - 1:w], ps[v][:, p * P:(p + 1) * P],
                                                       ALU.mult, ALU.add)
                        if p == NP - 1:
                            ins.then_inc(sem("state_dn"), 1)
                        else:
                            step(ins, wait=False)
                    dve.wait_ge(sem("b_step"), step.value())
                    dve.wait_ge(sem("state_dn"), c + 1)

                def between():
                    dve.wait_ge(sem("zeroed"), 15)

                go(dve, {"S": lambda ch: None, "W": lambda ch: None, "fD": fD, "fM": fM, "L": L, "rM": rM, "rD": rD}, between, step)
        if upto < 3:
            return
        clear_semaphores()

        sumr, root = rows[:, 0, :], rows[:, 1, :]
        ring4 = ring + [ext[:, 0:KT * P]]
        memv = zml[:, 6:9, :].rearrange("p k t -> p (k t)")[:, 0:KT * NMEM].rearrange("p (k t) -> p k t", k=KT)
        wk = [regH[:, n * KT * P:(n + 1) * KT * P] for n in range(XH)]
        wv = regH[:, 4096:8192].rearrange("p (k n) -> p k n", k=KT)
        mkT = qkv[:, 7, 0:XH * NMEM].rearrange("p (h m) -> p h m", h=XH)
        mv = qkv[:, 8, 0:2 * XH * XD].rearrange("p (m n) -> p m n", m=2)
        qT, oT = zml[:, 0:4, :], zml[:, 4:8, :]
        prob, probT, qfix = zml[:, 8, 0:1024], zml[:, 9, 0:1024], zml[:, 10, 0:512].rearrange("p (h t) -> p h t", h=XH)
        qm = acc[:, 0:1024].rearrange("p (b h t) -> p b h t", b=DB, h=XH)
        stat = small[:, 4:16].rearrange("p (n h) -> p n h", n=3)
        kc, vc = [qkv[:, 3 + k, 0:1024] for k in range(2)], [qkv[:, 5 + k, 0:1024] for k in range(2)]
        relus = feat[:, 3 * KT, :]
        feat_r, regH_r = rounded("feat", [P, 17 + CONV, T]), rounded("regH", [P, KT, T])
        regW_r, ext_r, rows_r = rounded("regW", [P, 3 * KT * P]), rounded("ext", [P, EXT]), rounded("rows", [P, 2, T])
        h_hi, h_lo = feat_r[:, 0:KT, :], regH_r[:, :, :]
        hid_hi, hid_lo, hid = feat_r[:, KT:2 * KT, :], feat_r[:, 2 * KT:3 * KT, :], feat[:, 2 * KT:3 * KT, :]
        w_hi = [rows_r[:, k, 0:KT * P] for k in range(2)]
        w_lo = [regW_r[:, k * KT * P:(k + 1) * KT * P] for k in range(3)] + [ext_r[:, 0:KT * P]]
        mixed = [qkv[:, k, :] for k in range(3)] + [zml[:, k, :] for k in range(3)] + [u[:, k, :] for k in range(2)]
        SCALE = float(XD) ** -0.5
        N_OUT, N_Q, N_O, N_F = 0, KT, KT + XH, 2 * KT + XH
        NT = N_F + 2 * FT

        def sums(r):
            return feat[:, 0, :] if r == 2 else sumr

        for n in ("xr_in mem_in wk_in wv_in m_sq m_sum m_ps m_root m_h mix_sq mix_ps mix_root mix_v mix_done mix_gate mix_n "
                  "gelu glu_w glu_ps glu_sig glu_done mk_ps mk_out mv_ps mv_out r0 r1 r2 r3 gg ge n_sq n_sum n_ps n_root n_h "
                  "v_step t_step qfix_ready at_s at_max at_exp at_p at_tp at_t at_o at_out qm_zero qm_ready kc0 kc1 vc0 vc1 "
                  "sc_s sc_max sc_exp sc_p sc_tp sc_t sc_o sc_out y_out relu k_done v_done inv_at inv_sc mem_out h_hi h_lo w_hi w_lo squared hid_lo").split():
            sem(n)

        with nc.Block() as block:
            @block.sync
            def _(q):
                q.dma_start(memv, t["memT"]).then_inc(sem("mem_in"), 16)
                for n in range(XH):
                    q.dma_start(wk[n], t["w_xk"][n]).then_inc(sem("wk_in"), 16)
                q.dma_start(regH[:, 4096:8192], t["w_xv"][0]).then_inc(sem("wv_in"), 16)
                q.dma_start(acc[:, 0:512].rearrange("p (n c) -> p n c", n=2), t["w_glu"].rearrange("n p c -> p n c"))\
                    .then_inc(sem("glu_w"), 16)
                q.dma_start(xv, t["xT"]).then_inc(sem("xr_in"), 16)

                def load(n, k, name, idx, w=KT * P, wait=True):
                    if wait:
                        q.wait_ge(sem("gg"), (n - 4) * 3 + (3 * k + 3))
                    q.dma_start(ring4[k][:, 0:w], t[name][idx]).then_inc(sem(f"r{k}"), 16)

                for n in range(KT):
                    load(n - n % 4, n % 4, "w_out", n, wait=n >= 4)
                for n in range(XH):
                    load(N_Q, n, "w_xq", n)
                for n in range(KT):
                    load(N_O + n - n % 4, n % 4, "w_xo", n, w=XH * P)
                with q.Fori(0, 4) as g:
                    for name, at in (("w_ff1", 0), ("w_ff2", 8)):
                        with q.Fori(0, 2) as j:
                            for k in range(4):
                                load(g * 16 + j * 4 + (N_F + at), k, name, g * 8 + j * 4 + k)
                for b in range(NB):
                    q.wait_ge(sem("n_h"), (2 * NB + b + 1) * KT)
                    q.dma_start(o["yT"][:, :, blk(b)], hv[:, :, blk(b)]).then_inc(sem("y_out"), 16)
                q.wait_ge(sem("y_out"), 48)

            @block.gpsimd
            def _(pool):
                pool.wait_ge(sem("mk_out"), XH)
                pool.dma_start(o["mkT"], mkT).then_inc(sem("mem_out"), 16)
                pool.wait_ge(sem("mv_out"), 2)
                pool.dma_start(o["mv"], mv).then_inc(sem("mem_out"), 16)
                pool.wait_ge(sem("glu_done"), 6)
                for b in range(DB):
                    if b >= 2:
                        pool.wait_ge(sem("k_done"), b - 1)
                    pool.dma_start(kc[b % 2], t["ck"][:, b, :]).then_inc(sem(f"kc{b % 2}"), 16)
                    if b < 2:
                        pool.dma_start(vc[b % 2], t["cv"][:, b, :]).then_inc(sem(f"vc{b % 2}"), 16)
                for b in range(2, DB):
                    pool.wait_ge(sem("v_done"), b - 1)
                    pool.dma_start(vc[b % 2], t["cv"][:, b, :]).then_inc(sem(f"vc{b % 2}"), 16)
                pool.wait_ge(sem("mem_out"), 32)

                with pool.Fori(0, 4 * 4) as m:
                    for k in range(4):
                        if k == 0:
                            pool.wait_ge(sem("n_ps"), 2 * NB)
                        elif k == 1:
                            pool.wait_ge(sem("n_h"), 2 * NB * KT)
                        pool.wait_ge(sem(f"r{k}"), m * 16 + 16 * 6)
                        pool.wait_ge(sem("gg"), m * 12 + (N_F + k - 1) * 3)
                        pool.tensor_tensor(w_hi[k % 2], ring4[k], ones[:, 0:1].to_broadcast([P, KT * P]), ALU.mult).then_inc(sem("w_hi"), 1)
                        pool.wait_ge(sem("w_hi"), m * 4 + (k + 1))
                        pool.tensor_tensor(w_lo[k], ring4[k], w_hi[k % 2], ALU.subtract).then_inc(sem("w_lo"), 1)

            @block.tensor
            def _(pe):
                pe.wait_ge(sem("m_sum"), KT)
                pe.matmul(ps[5][:, 0:NMEM], ones, sumr[:, 0:NMEM], start=True, stop=True).then_inc(sem("m_ps"), 1)

                def mix_sums(j):
                    pe.wait_ge(sem("mix_sq"), j + 1)
                    for b in range(NB):
                        i = j * NB + b
                        if i >= 2:
                            pe.wait_ge(sem("mix_v"), i - 1)
                        pe.matmul(ps[6 + i % 2][:, 0:BW], heads, qkv[:, 3 + j % 2, blk(b)], start=True, stop=True)\
                          .then_inc(sem("mix_ps"), 1)

                mix_sums(0)
                mix_sums(1)
                pe.wait_ge(sem("m_h"), KT)
                pe.wait_ge(sem("wk_in"), 16 * XH)
                for n in range(XH):
                    for k in range(KT):
                        ins = pe.matmul(ps[n // 2][:, (n % 2) * NMEM:(n % 2 + 1) * NMEM], wk[n][:, k * P:(k + 1) * P], memv[:, k, :],
                                        start=(k == 0), stop=(k == KT - 1))
                    if n % 2:
                        ins.then_inc(sem("mk_ps"), 1)
                mix_sums(2)
                pe.wait_ge(sem("wv_in"), 16)
                for m in range(2):
                    for k in range(KT):
                        ins = pe.matmul(ps[3 + m][:, :], memv[:, k, m * P:(m + 1) * P], wv[:, k, :],
                                        start=(k == 0), stop=(k == KT - 1))
                    ins.then_inc(sem("mv_ps"), 1)
                for j in (3, 4, 5):
                    mix_sums(j)
                pe.wait_ge(sem("gelu"), 2)
                pe.wait_ge(sem("glu_w"), 16)
                for n in range(2):
                    for b in range(NB):
                        i = n * NB + b
                        if i >= 2:
                            pe.wait_ge(sem("glu_sig"), i - 1)
                        if i < 2:
                            pe.wait_ge(sem("mv_out"), 2)
                        for k in range(2):
                            ins = pe.matmul(ps[3 + i % 2][:, 0:BW], acc[:, n * 256 + k * P:n * 256 + (k + 1) * P], u[:, k, blk(b)],
                                            start=(k == 0), stop=(k == 1))
                        ins.then_inc(sem("glu_ps"), 1)

                def gemm(n, slot, loads, rhs, kt=KT, first=False, blocks=False):
                    pe.wait_ge(sem(f"r{slot}"), loads * 16)
                    for b in range(NB):
                        if not first:
                            pe.wait_ge(sem("ge"), n * 3 + (b - 2))
                        if blocks:
                            pe.wait_ge(sem("n_h"), (b + 1) * KT)
                        for k in range(kt):
                            ins = pe.matmul(ps[b][:, 0:BW], ring4[slot][:, k * P:(k + 1) * P], rhs(k, b),
                                            start=(k == 0), stop=(k == kt - 1))
                        ins.then_inc(sem("gg"), 1)

                pe.wait_ge(sem("mix_done"), 6)
                pe.wait_ge(sem("glu_done"), 6)
                pe.wait_ge(sem("mk_out"), XH)
                for n in range(KT):
                    gemm(n, n % 4, n // 4 + 1, lambda k, b: mixed[k][:, blk(b)], first=n == 0)

                def norm(r):
                    for b in range(NB):
                        pe.wait_ge(sem("n_sum"), (r * KT + KT - 1) * NB + b + 1)
                        i = r * NB + b
                        if b >= 2:
                            pe.wait_ge(sem("n_root"), i - 1)
                        pe.matmul(ps[6 + b % 2][:, 0:BW], ones, sums(r)[:, blk(b)], start=True, stop=True).then_inc(sem("n_ps"), 1)

                norm(0)
                for n in range(XH):
                    gemm(N_Q + n, n, 3, lambda k, b: hv[:, k, blk(b)], blocks=n == 0)

                def scores(i):
                    pe.wait_ge(sem("qfix_ready"), i + 1)
                    for h in range(XH):
                        ins = pe.matmul(ps[h // 2][:, (h % 2) * NMEM:(h % 2 + 1) * NMEM], qfix[:, h, :], mkT[:, h, :], start=True, stop=True)
                    ins.then_inc(sem("at_s"), 1)

                def weighted(i):
                    pe.wait_ge(sem("at_p"), i + 1)
                    for h in range(XH):
                        for m in range(2):
                            ins = pe.transpose(ps[2 + h // 2][:, (h % 2) * 256 + m * P:(h % 2) * 256 + (m + 1) * P],
                                               prob[:, h * NMEM + m * P:h * NMEM + (m + 1) * P], ident)
                    ins.then_inc(sem("at_tp"), 1)
                    pe.wait_ge(sem("at_t"), i * 2 + 2)
                    for h in range(XH):
                        for m in range(2):
                            ins = pe.matmul(ps[4][:, h * P:(h + 1) * P], mv[:, m, h * XD:(h + 1) * XD],
                                            probT[:, h * 256 + m * P:h * 256 + (m + 1) * P], start=(m == 0), stop=(m == 1))
                    ins.then_inc(sem("at_o"), 1)

                pe.wait_ge(sem("ge"), N_O * 3)
                scores(0)
                weighted(0)
                with pe.Fori(1, SEQ // P) as i:
                    pe.wait_ge(sem("at_exp"), i * XH)
                    scores(i)
                    pe.wait_ge(sem("at_out"), i * 1)
                    weighted(i)

                pe.wait_ge(sem("qm_ready"), DB)
                pe.wait_ge(sem("at_exp"), XH * (SEQ // P))
                pe.wait_ge(sem("at_t"), 2 * (SEQ // P))
                for b in range(DB):
                    pe.wait_ge(sem(f"kc{b % 2}"), 16 * (b // 2 + 1))
                    for h in range(XH):
                        ins = pe.matmul(ps[h][0:DB * DS, 0:NMEM], qm[:, b, h, :], kc[b % 2][:, h * NMEM:(h + 1) * NMEM],
                                        start=(b == 0), stop=(b == DB - 1))
                    ins.then_inc(sem("k_done"), 1)
                pe.wait_ge(sem("sc_p"), 1)
                for h in range(XH):
                    for m in range(2):
                        ins = pe.transpose(ps[5][:, (h * 2 + m) * 32:(h * 2 + m + 1) * 32],
                                           prob[0:32, h * NMEM + m * P:h * NMEM + (m + 1) * P], ident[0:32, 0:32])
                ins.then_inc(sem("sc_tp"), 1)
                pe.wait_ge(sem("sc_t"), 1)
                pe.wait_ge(sem("at_out"), SEQ // P)
                for b in range(DB):
                    pe.wait_ge(sem(f"vc{b % 2}"), 16 * (b // 2 + 1))
                    for h in range(XH):
                        for m in range(2):
                            at = (h * 2 + m) * 32 + b * DS
                            ins = pe.matmul(ps[4][:, h * 32 + b * DS:h * 32 + (b + 1) * DS],
                                            vc[b % 2][:, m * 512 + h * XD:m * 512 + (h + 1) * XD], probT[:, at:at + DS],
                                            start=(m == 0), stop=(m == 1))
                    ins.then_inc(sem("v_done"), 1)

                pe.wait_ge(sem("sc_out"), 1)
                pe.wait_ge(sem("sc_exp"), XH)
                for n in range(KT):
                    gemm(N_O + n, n % 4, 4 + n // 4, lambda k, b: oT[:, k, blk(b)], kt=XH)
                norm(1)
                def gemm_split(n, slot, rhs_hi, rhs_lo):
                    pe.wait_ge(sem("w_lo"), n - (N_F - 1))
                    for b in range(NB):
                        pe.wait_ge(sem("ge"), n * 3 + (b - 2))
                        pe.wait_ge(sem("h_lo"), (b + 1) * KT)
                        for k in range(KT):
                            hi, lo = w_hi[slot % 2][:, k * P:(k + 1) * P], w_lo[slot][:, k * P:(k + 1) * P]
                            pe.matmul(ps[b][:, 0:BW], hi, rhs_hi(k, b), start=(k == 0), stop=False)
                            pe.matmul(ps[b][:, 0:BW], hi, rhs_lo(k, b), start=False, stop=False)
                            ins = pe.matmul(ps[b][:, 0:BW], lo, rhs_hi(k, b), start=False, stop=(k == KT - 1))
                        ins.then_inc(sem("gg"), 1)

                with pe.Fori(0, 4) as g:
                    with pe.Fori(0, 2) as j:
                        for k4 in range(4):
                            gemm_split(g * 16 + j * 4 + (N_F + k4), k4, lambda k, b: h_hi[:, k, blk(b)], lambda k, b: h_lo[:, k, blk(b)])
                    with pe.Fori(0, 2) as j:
                        pe.wait_ge(sem("hid_lo"), g * 24 + 24)
                        for k4 in range(4):
                            gemm_split(g * 16 + j * 4 + (N_F + 8 + k4), k4, lambda k, b: hid_hi[:, k, blk(b)], lambda k, b: hid_lo[:, k, blk(b)])
                norm(2)

            @block.scalar
            def _(act):
                step = Steps(act, sem("t_step"))
                act.wait_ge(sem("mem_in"), 16)
                for k in range(KT):
                    if k >= 2:
                        act.wait_ge(sem("m_sum"), k - 1)
                    act.activation(root[:, (k % 2) * NMEM:(k % 2 + 1) * NMEM], memv[:, k, :], ACT.Square).then_inc(sem("m_sq"), 1)
                for j in range(6):
                    x_ = mixed[j]
                    if j >= 2:
                        act.wait_ge(sem("mix_ps"), (j - 1) * NB)
                    act.activation(qkv[:, 3 + j % 2, :], x_, ACT.Square).then_inc(sem("mix_sq"), 1)
                    if j == 0:
                        act.wait_ge(sem("m_ps"), 1)
                        act.activation(root[:, 512:512 + NMEM], ps[5][:, 0:NMEM], ACT.Sqrt, bias=pcol("eps"), scale=1.0 / D)\
                           .then_inc(sem("m_root"), 1)
                    if j >= 3:
                        step(act.activation(zml[:, j, :], zml[:, j, :], ACT.Square, scale=EPS ** 0.5))
                    if j in (2, 3):
                        for h in range(2):
                            act.wait_ge(sem("mk_ps" if j == 2 else "mv_ps"), h + 1)
                            if j == 2:
                                act.activation(mkT[:, 2 * h:2 * h + 2, :], ps[h][:, :].rearrange("p (n m) -> p n m", n=2), ACT.Copy)\
                                   .then_inc(sem("mk_out"), 2)
                            else:
                                act.activation(mv[:, h, :], ps[3 + h][:, :], ACT.Copy).then_inc(sem("mv_out"), 1)
                    for b in range(NB):
                        act.wait_ge(sem("mix_v"), j * NB + b + 1)
                        v = qkv[:, 5 + j % 2, blk(b)]
                        act.activation(v, v, ACT.Sqrt).then_inc(sem("mix_root"), 1)
                for j in range(6):
                    g = zg[:, j, :] if j < 3 else zml[:, 6 + j, :]
                    act.activation(g, g, ACT.Silu if j < 3 else ACT.Sigmoid).then_inc(sem("mix_gate"), 1)
                for k in range(2):
                    act.activation(u[:, k, :], u[:, k, :], ACT.Gelu_apprx_tanh).then_inc(sem("gelu"), 1)
                for n in range(2):
                    for b in range(NB):
                        act.wait_ge(sem("glu_ps"), n * NB + b + 1)
                        act.activation(qkv[:, 3 + n, blk(b)], ps[3 + (n * NB + b) % 2][:, 0:BW], ACT.Sigmoid, bias=pcol("glu", n))\
                           .then_inc(sem("glu_sig"), 1)

                def norm(r, ready):
                    for k in range(KT):
                        act.wait_ge(sem("ge"), ready(k))
                        for b in range(NB):
                            n = (r * KT + k) * NB + b
                            if n >= 3:
                                act.wait_ge(sem("n_sum"), n - 2)
                            act.activation(acc[:, blk(b)], xv[:, k, blk(b)], ACT.Square).then_inc(sem("n_sq"), 1)
                    for b in range(NB):
                        act.wait_ge(sem("n_ps"), r * NB + b + 1)
                        act.activation(root[:, blk(b)], ps[6 + b % 2][:, 0:BW], ACT.Sqrt, bias=pcol("eps"), scale=1.0 / D)\
                           .then_inc(sem("n_root"), 1)

                def evac(n, b, dst):
                    act.wait_ge(sem("gg"), n * 3 + (b + 1))
                    act.activation(dst, ps[b][:, 0:BW], ACT.Copy).then_inc(sem("ge"), 1)

                def evac_relu(n, b, squares, at):
                    act.wait_ge(sem("gg"), n * 3 + (b + 1))
                    if b > 0:
                        act.wait_ge(sem("relu"), squares + b)
                    act.activation(relus[:, blk(b)], ps[b][:, 0:BW], ACT.Relu).then_inc(sem("ge"), 1)
                    act.wait_ge(sem("ge"), n * 3 + (b + 1))
                    act.activation(hid[:, at, blk(b)], relus[:, blk(b)], ACT.Square).then_inc(sem("squared"), 1)
                    act.wait_ge(sem("squared"), squares + (b + 1))
                    act.activation(hid_hi[:, at, blk(b)], hid[:, at, blk(b)], ACT.Copy).then_inc(sem("relu"), 1)

                act.wait_ge(sem("glu_done"), 6)
                norm(0, lambda k: (N_OUT + k + 1) * 3)
                for n in range(XH):
                    for b in range(NB):
                        evac(N_Q + n, b, qT[:, n, blk(b)])
                act.wait_ge(sem("ge"), N_O * 3)

                def tile(i):
                    if is_first(i):
                        pass
                    else:
                        act.wait_ge(sem("at_s"), i * 1)
                        alone(act, i, sem("mem_in"), 16)
                    act.activation(qfix, qT[:, :, bass.ts(i, P)], ACT.Copy).then_inc(sem("qfix_ready"), 1)
                    act.wait_ge(sem("at_max"), i + 1)
                    if not is_first(i):
                        act.wait_ge(sem("at_tp"), i * 1)
                    for h in range(XH):
                        act.activation(prob[:, h * NMEM:(h + 1) * NMEM], ps[h // 2][:, (h % 2) * NMEM:(h % 2 + 1) * NMEM], ACT.Exp,
                                       bias=stat[:, 0, h:h + 1], scale=SCALE, accum_out=stat[:, 1, h:h + 1]).then_inc(sem("at_exp"), 1)
                    act.wait_ge(sem("at_tp"), i + 1)
                    if not is_first(i):
                        act.wait_ge(sem("at_o"), i * 1)
                    for h in range(2):
                        act.activation(probT[:, h * 512:(h + 1) * 512], ps[2 + h][:, :], ACT.Copy).then_inc(sem("at_t"), 1)
                    act.wait_ge(sem("at_o"), i + 1)
                    alone(act, i, sem("mem_in"), 16)
                    act.activation(oT[:, :, bass.ts(i, P)], ps[4][:, :].rearrange("p (h t) -> p h t", h=XH), ACT.Copy)\
                       .then_inc(sem("at_out"), 1)

                tile(0)
                with act.Fori(1, SEQ // P) as i:
                    tile(i)
                act.wait_ge(sem("sc_max"), 1)
                for h in range(XH):
                    act.activation(prob[0:32, h * NMEM:(h + 1) * NMEM], ps[h][0:32, 0:NMEM], ACT.Exp,
                                   bias=stat[0:32, 0, h:h + 1], scale=SCALE, accum_out=stat[0:32, 1, h:h + 1]).then_inc(sem("sc_exp"), 1)
                act.wait_ge(sem("sc_tp"), 1)
                act.activation(probT[:, 0:256], ps[5][:, 0:256], ACT.Copy).then_inc(sem("sc_t"), 1)
                act.wait_ge(sem("v_done"), DB)
                act.activation(oT[:, :, SEQ:T], ps[4][:, 0:XH * 32].rearrange("p (h t) -> p h t", h=XH), ACT.Copy)\
                   .then_inc(sem("sc_out"), 1)
                norm(1, lambda k: (N_O + k + 1) * 3)
                for b in range(NB):
                    for k in range(KT):
                        act.wait_ge(sem("n_h"), (NB + b) * KT + k + 1)
                        act.activation(h_hi[:, k, blk(b)], hv[:, k, blk(b)], ACT.Copy).then_inc(sem("h_hi"), 1)
                with act.Fori(0, 4) as g:
                    with act.Fori(0, 2) as j:
                        act.wait_ge(sem("ge"), g * 48 + N_F * 3)
                        for k in range(4):
                            for b in range(NB):
                                n = g * 16 + j * 4 + (N_F + k)
                                evac_relu(n, b, g * 24 + j * 12 + k * 3, j * 4 + k)
                norm(2, lambda k: (NT - KT + k + 1) * 3)

            @block.vector
            def _(dve):
                step = Steps(dve, sem("v_step"))
                for k in range(KT):
                    dve.wait_ge(sem("m_sq"), k + 1)
                    sq = root[:, (k % 2) * NMEM:(k % 2 + 1) * NMEM]
                    if k == 0:
                        dve.tensor_copy(sumr[:, 0:NMEM], sq).then_inc(sem("m_sum"), 1)
                    else:
                        dve.tensor_tensor(sumr[:, 0:NMEM], sumr[:, 0:NMEM], sq, ALU.add).then_inc(sem("m_sum"), 1)
                    dve.wait_ge(sem("m_sum"), k + 1)
                dve.wait_ge(sem("m_root"), 1)
                step(dve.reciprocal(root[:, 768:768 + NMEM], root[:, 512:512 + NMEM]))
                for k in range(KT):
                    dve.scalar_tensor_tensor(memv[:, k, :], memv[:, k, :], pcol("mem", k), root[:, 768:768 + NMEM], ALU.mult, ALU.mult)\
                       .then_inc(sem("m_h"), 1)
                for j in range(6):
                    for b in range(NB):
                        i = j * NB + b
                        v = qkv[:, 5 + j % 2, blk(b)]
                        dve.wait_ge(sem("mix_ps"), i + 1)
                        pss = ps[6 + i % 2][:, 0:BW]
                        if j < 3:
                            dve.tensor_scalar(v, pss, 1.0 / HD, EPS, ALU.mult, ALU.add).then_inc(sem("mix_v"), 1)
                        else:
                            if b == 0:
                                dve.wait_ge(sem("t_step"), j - 2)
                            step(dve.scalar_tensor_tensor(v, pss, 1.0 / HD, zml[:, j, blk(b)], ALU.mult, ALU.add))
                            dve.tensor_scalar(v, v, 1e-34, None, ALU.max).then_inc(sem("mix_v"), 1)
                    for b in range(NB):
                        i = j * NB + b
                        v = qkv[:, 5 + j % 2, blk(b)]
                        dve.wait_ge(sem("mix_root"), i + 1)
                        step(dve.reciprocal(v, v))
                        x_ = mixed[j][:, blk(b)]
                        step(dve.scalar_tensor_tensor(x_, x_, pcol("dn" if j < 3 else "ml"), v, ALU.mult, ALU.mult), wait=b == 2)
                for j in range(6):
                    dve.wait_ge(sem("mix_gate"), j + 1)
                    g = zg[:, j, :] if j < 3 else zml[:, 6 + j, :]
                    dve.tensor_tensor(mixed[j], mixed[j], g, ALU.mult).then_inc(sem("mix_done"), 1)
                dve.wait_ge(sem("glu_sig"), 6)
                for n in range(2):
                    for b in range(NB):
                        dve.tensor_tensor(u[:, n, blk(b)], u[:, n, blk(b)], qkv[:, 3 + n, blk(b)], ALU.mult).then_inc(sem("glu_done"), 1)
                dve.wait_ge(sem("xr_in"), 16)

                def residual(n, b, dst):
                    dve.wait_ge(sem("gg"), n * 3 + (b + 1))
                    dve.tensor_tensor(dst, ps[b][:, 0:BW], dst, ALU.add).then_inc(sem("ge"), 1)

                def add_squares(r, k):
                    for b in range(NB):
                        n = (r * KT + k) * NB + b
                        dve.wait_ge(sem("n_sq"), n + 1)
                        if k == 0:
                            dve.tensor_copy(sums(r)[:, blk(b)], acc[:, blk(b)]).then_inc(sem("n_sum"), 1)
                        else:
                            dve.wait_ge(sem("n_sum"), n - 2)
                            dve.tensor_tensor(sums(r)[:, blk(b)], sums(r)[:, blk(b)], acc[:, blk(b)], ALU.add).then_inc(sem("n_sum"), 1)

                def norm(r, name):
                    add_squares(r, KT - 1)
                    for b in range(NB):
                        dve.wait_ge(sem("n_root"), r * NB + b + 1)
                        step(dve.reciprocal(root[:, blk(b)], root[:, blk(b)]))
                        for k in range(KT):
                            dve.scalar_tensor_tensor(hv[:, k, blk(b)], xv[:, k, blk(b)], pcol(name, k), root[:, blk(b)],
                                                     ALU.mult, ALU.mult).then_inc(sem("n_h"), 1)
                        if r == 1:
                            for k in range(KT):
                                dve.wait_ge(sem("h_hi"), b * KT + k + 1)
                                dve.tensor_tensor(h_lo[:, k, blk(b)], hv[:, k, blk(b)], h_hi[:, k, blk(b)], ALU.subtract)\
                                   .then_inc(sem("h_lo"), 1)

                for n in range(KT):
                    for b in range(NB):
                        residual(n, b, xv[:, n, blk(b)])
                    if n > 0:
                        add_squares(0, n - 1)
                dve.wait_ge(sem("ge"), N_Q * 3)
                dve.wait_ge(sem("mv_ps"), 2)
                norm(0, "x")
                dve.wait_ge(sem("ge"), N_O * 3)

                def finish(r, s_inv, s_p, vi, vp, exp_sem, vexp):
                    dve.wait_ge(sem(exp_sem), vexp)
                    dve.reciprocal(stat[r, 2, :], stat[r, 1, :]).then_inc(sem(s_inv), 1)
                    dve.wait_ge(sem(s_inv), vi)
                    p = prob[r, :].rearrange("p (h m) -> p h m", h=XH)
                    dve.tensor_tensor(p, p, stat[r, 2, :].unsqueeze(2).to_broadcast([r.stop, XH, NMEM]), ALU.mult)\
                       .then_inc(sem(s_p), 1)
                    dve.wait_ge(sem(s_p), vp)

                def tile(i):
                    r = slice(0, P)
                    dve.wait_ge(sem("at_s"), i + 1)
                    for k in range(2):
                        src = ps[k][:, :].rearrange("p (h m) -> p h m", h=2)
                        step(dve.tensor_reduce(stat[:, 0, 2 * k:2 * k + 2], src, AX.X, ALU.max), wait=k == 1)
                    dve.tensor_scalar(stat[:, 0, :], stat[:, 0, :], -SCALE, None, ALU.mult).then_inc(sem("at_max"), 1)
                    finish(r, "inv_at", "at_p", i + 1, i + 1, "at_exp", i * XH + XH)

                n0 = step.n
                tile(0)
                per = step.n - n0
                with dve.Fori(1, SEQ // P) as i:
                    step.loop(i, per, 1)
                    tile(i)
                step.done(SEQ // P - 1, 1)
                dve.memset(acc[:, 0:1024], 0.0).then_inc(sem("qm_zero"), 1)
                dve.wait_ge(sem("qm_zero"), 1)
                for b in range(DB):
                    dve.tensor_copy(qm[:, b, :, b * DS:(b + 1) * DS], qT[:, :, SEQ + b * DS:SEQ + (b + 1) * DS]).then_inc(sem("qm_ready"), 1)
                dve.wait_ge(sem("k_done"), DB)
                for h in range(XH):
                    step(dve.tensor_reduce(stat[0:32, 0, h:h + 1], ps[h][0:32, 0:NMEM], AX.X, ALU.max), wait=h == XH - 1)
                dve.tensor_scalar(stat[0:32, 0, :], stat[0:32, 0, :], -SCALE, None, ALU.mult).then_inc(sem("sc_max"), 1)
                finish(slice(0, 32), "inv_sc", "sc_p", 1, 1, "sc_exp", XH)
                for n in range(KT):
                    for b in range(NB):
                        residual(N_O + n, b, xv[:, n, blk(b)])
                    if n > 0:
                        add_squares(1, n - 1)
                dve.wait_ge(sem("ge"), N_F * 3)
                norm(1, "ff")

                def split_hidden(g):
                    with dve.Fori(0, 2) as j:
                        for k in range(4):
                            for b in range(NB):
                                dve.wait_ge(sem("relu"), j * 12 + (g * 24 + k * 3 + b + 1))
                                at = j * 4 + k
                                dve.tensor_tensor(hid_lo[:, at, blk(b)], hid[:, at, blk(b)], hid_hi[:, at, blk(b)], ALU.subtract)\
                                   .then_inc(sem("hid_lo"), 1)

                with dve.Fori(0, 3) as g:
                    split_hidden(g)
                    with dve.Fori(0, 2) as j:
                        dve.wait_ge(sem("ge"), g * 48 + (N_F + 8) * 3)
                        for k in range(4):
                            for b in range(NB):
                                residual(g * 16 + j * 4 + (N_F + 8 + k), b, xv[:, j * 4 + k, blk(b)])
                split_hidden(3)
                dve.wait_ge(sem("ge"), (NT - KT) * 3)
                for n in range(KT):
                    for b in range(NB):
                        residual(NT - KT + n, b, xv[:, n, blk(b)])
                    if n > 0:
                        add_squares(2, n - 1)
                norm(2, "final")


def constants():
    c = np.zeros((P, NCC), np.float32)

    def put(name, a):
        a = np.asarray(a, np.float32).reshape(a.shape[0], -1)
        c[:a.shape[0], CC[name]:CC[name] + a.shape[1]] = a

    half = np.arange(P) // 64
    place = np.arange(P) % 64
    put("ident", np.eye(P))
    put("ones", np.ones((P, P)))
    same = (half[:, None] == half[None, :]).astype(np.float32)
    put("heads", same)
    sel = np.zeros((P, 5, 3, P), np.float32)
    for q, (base, _) in enumerate(ROWS):
        for p in range(3):
            for m in range(P):
                sel[base + 2 * p + half[m], q, p, m] = 1
    put("rowsel", sel)
    col = np.zeros((P, 2, 2, 9), np.float32)
    for h in range(2):
        for q, (base, tile) in enumerate(COLS):
            for p in range(3):
                col[base + 2 * p + h, h, tile, q * 3 + p] = 1
    put("colsel", col)
    put("causal", np.broadcast_to(np.where(place[:, None] > np.arange(64)[None, :], -BIG, 0.0)[:, None, :], (P, 3, 64)))
    off = np.zeros((P, 6, 3, P), np.float32)
    for n in range(6):
        b = 1 << n
        r, q = place[:, None], place[None, :]
        m = same * (r // (2 * b) == q // (2 * b)) * (r % (2 * b) < b) * (q % (2 * b) >= b)
        off[:, n] = -m[:, None, :]
    put("off", off)
    put("eye3", np.broadcast_to(np.eye(P)[:, None, :], (P, 3, P)))
    put("blk3", np.broadcast_to(same[:, None, :], (P, 3, P)))
    cmask = np.ones((H, SEQ), np.float32)
    cmask[:, ::CW] = 0
    resets = np.ones((P, DB * DS), np.float32)
    resets[:, ::DS] = 0
    return c, cmask, resets


def lay_out(x):
    f = np.float32
    x = {k: np.asarray(v) for k, v in x.items()}

    def tiles(w, cols):
        k, n = w.shape
        return np.ascontiguousarray(w.reshape(k // P, P, n // cols, cols).transpose(2, 1, 0, 3)).reshape(n // cols, P, -1)

    def feat(v, n):
        return v.reshape(n, P).T

    a = {}
    xt = np.concatenate([x["x_prompt"].reshape(SEQ, D), x["x_sample"].reshape(DB * DS, D)], 0)
    a["xT"] = np.ascontiguousarray(xt.T.reshape(KT, P, T).transpose(1, 0, 2))
    a["memT"] = np.ascontiguousarray(x["mem_prompt"].reshape(NMEM, D).T.reshape(KT, P, NMEM).transpose(1, 0, 2))
    w = x["w_in"][0]
    sizes = [384, 384, 384, 6, 6, 384, 384, 384, 384, 6, 6, 384, 256]
    cuts = np.cumsum([0] + sizes)
    part = {n: w[:, cuts[k]:cuts[k + 1]] for k, n in enumerate(("q", "k", "v", "beta", "alpha", "gate", "lq", "lk", "lv", "li", "lf", "lo", "u"))}
    gates = np.zeros((D, P), f)
    for k, n in enumerate(("beta", "alpha", "li", "lf")):
        gates[:, 32 * k:32 * k + 6] = part[n]
    def cut(m, k):
        return m[:, k * P:(k + 1) * P]
    ml = np.concatenate([part[n] for n in ("lq", "lk", "lv", "lo")], 1)
    qk = np.concatenate([part["q"], part["k"]], 1)
    cols = [cut(part["u"], 0), cut(part["u"], 1), gates]
    for i in range(6):
        cols += [cut(qk, i), cut(ml, 2 * i), cut(ml, 2 * i + 1)]
    for i in range(3):
        cols += [cut(part["v"], i), cut(part["gate"], i)]
    a["w_in"] = tiles(np.concatenate(cols, 1), P)
    a["w_out"] = tiles(x["w_out"][0], P)
    a["w_xq"] = tiles(x["w_xq"][0], P)
    a["w_xk"] = tiles(x["w_xk"][0], P)
    a["w_xv"] = tiles(x["w_xv"][0], 512)
    a["w_xo"] = tiles(x["w_xo"][0], P)
    a["w_ff1"] = tiles(x["w_ff1"][0], P)
    w2 = x["w_ff2"][0].reshape(4, D, D)
    a["w_ff2"] = np.concatenate([tiles(w2[g], P) for g in range(4)], 0)
    a["w_glu"] = tiles(x["s5_w_glu"][0], P)
    par = np.zeros((P, NPC), f)

    def put(name, v, rows=slice(0, P)):
        v = v.reshape(v.shape[0], -1)
        par[rows, PC[name]:PC[name] + v.shape[1]] = v

    for n, k in (("mix", "norm_mix"), ("x", "norm_x"), ("ff", "norm_ff"), ("mem", "norm_mem")):
        put(n, feat(x[k][0], KT))
    put("final", feat(x["norm_final"], KT))
    put("conv", x["dn_conv_w"][0].T.reshape(CONV, P, 4).transpose(1, 0, 2))
    put("dn", np.tile(x["dn_norm"][0], 2)[:, None])
    put("ml", np.tile(x["ml_norm"][0], 2)[:, None])
    d = np.ones((ST, P), f)
    for s in range(ST):
        c = 32 * (s % 4)
        d[s, c:c + 32] = x["s5_d"][0].reshape(-1)[32 * s:32 * s + 32]
    put("dsel", d.T)
    put("glu", feat(x["s5_b_glu"][0], 2))
    put("lr", feat(x["s5_lam_re"][0].reshape(-1), ST))
    put("li", feat(x["s5_lam_im"][0].reshape(-1), ST))
    put("ldt", np.repeat(x["s5_log_dt"][0], 64).reshape(ST, P).T)
    for k, n in ((1, "dn_dt_bias"), (2, "ml_i_bias"), (3, "ml_f_bias")):
        put("bias", x[n][0][:, None], slice(32 * k, 32 * k + 6))
    put("alog", x["dn_a_log"][0][:, None], slice(0, 6))
    put("m0", x["state_ml_m"][0].T, slice(0, 6))
    put("eps", np.full((P, 1), EPS, f))
    put("halfpi", np.full((P, 1), HALF_PI, f))
    put("one", np.ones((P, 1), f))
    a["par"] = par
    b = np.zeros((ST, P, 2, P), f)
    c = np.zeros((ST, P, 2, P), f)
    for s in range(ST):
        for g in range(2):
            at = 32 * (s % 4) + 16 * g
            r = slice(64 * g, 64 * g + 64)
            for k, (nb, ncc) in enumerate((("s5_b_re", "s5_c_re"), ("s5_b_im", "s5_c_im"))):
                b[s, r, k, at:at + 16] = x[nb][0, 2 * s + g]
                c[s, r, k, at:at + 16] = x[ncc][0, 2 * s + g].T
    a["s5_b"], a["s5_c"] = b.reshape(ST, P, 256), c.reshape(ST, P, 256).transpose(1, 0, 2).copy()
    h = np.stack([x["state_ssm_re"][0], x["state_ssm_im"][0]])
    a["h0"] = np.ascontiguousarray(h.reshape(2, DB, ST, P).transpose(3, 0, 2, 1))
    a["cstate"] = np.ascontiguousarray(x["state_dn_conv"][0].transpose(2, 0, 1).reshape(CONV, P, 3 * DB).transpose(1, 0, 2))

    def bd(s):
        out = np.zeros((s.shape[0], P, NP, P), f)
        for p in range(NP):
            for g in range(2):
                out[:, 64 * g:64 * g + 64, p, 64 * g:64 * g + 64] = s[:, 2 * p + g]
        return out.reshape(s.shape[0], P, NP * P)

    a["dn_s0"] = bd(x["state_dn_s"][0])
    a["ml_c0"] = bd(x["state_ml_c"][0])
    a["ml_n0"] = bd(np.repeat(x["state_ml_n"][0][..., None], 64, -1))
    k = x["cache_mem_k"][0].transpose(3, 0, 2, 1)
    a["ck"] = np.ascontiguousarray(k).reshape(P, DB, XH * NMEM)
    v = x["cache_mem_v"][0].reshape(DB, 2, P, XH * XD).transpose(2, 0, 1, 3)
    a["cv"] = np.ascontiguousarray(v).reshape(P, DB, 2 * XH * XD)
    a["cst"], a["cmask"], a["resets"] = constants()
    return a


ROWS = ((0, 0), (32, 0), (64, 0), (96, 0), (0, 1))
COLS = ((0, 0), (32, 0), (32, 1))

OUTS = {"hend": (P, 2, ST, 1 + DB), "mend": (H, 1 + DB), "cnew": (P, CONV, 3 + 3 * DB),
        "yT": (P, KT, T), "dn_s": (1 + DB, P, NP, P), "ml_c": (1 + DB, P, NP, P), "ml_n": (1 + DB, P, NP, P),
        "mkT": (P, XH, NMEM), "mv": (P, 2, XH * XD)}


def kernel(**inputs):
    import concourse.bacc as bacc
    from concourse.bass_utils import run_bass_kernel_spmd

    nc = bacc.Bacc("TRN2", target_bir_lowering=False, num_devices=1)
    arrays = lay_out(inputs)
    ins = {k: nc.dram_tensor(f"{k}_in", v.shape, F32, kind="ExternalInput").ap() for k, v in arrays.items()}
    outs = {k: nc.dram_tensor(f"{k}_out", v, F32, kind="ExternalOutput").ap() for k, v in OUTS.items()}
    build(nc, ins, outs)
    r = run_bass_kernel_spmd(nc, [{f"{k}_in": v for k, v in arrays.items()}], core_ids=[0]).results[0]
    g = {k: np.asarray(r[f"{k}_out"]) for k in OUTS}

    y = g["yT"].transpose(1, 0, 2).reshape(D, T).T
    conv = g["cnew"].transpose(1, 0, 2).reshape(CONV * P, 1 + DB, 3).transpose(1, 2, 0)

    def heads(s):
        out = np.empty((s.shape[0], H, 64, 64), np.float32)
        for p in range(NP):
            for k in range(2):
                out[:, 2 * p + k] = s[:, 64 * k:64 * k + 64, p, 64 * k:64 * k + 64]
        return out

    dn, mc, mn = heads(g["dn_s"]), heads(g["ml_c"]), heads(g["ml_n"])[..., 0]
    mm = g["mend"].T
    hh = g["hend"].transpose(1, 3, 2, 0).reshape(2, 1 + DB, 16, 64)
    mk = g["mkT"].transpose(2, 1, 0)
    mv = g["mv"].transpose(1, 0, 2).reshape(NMEM, XH, XD)

    def c(v):
        return np.ascontiguousarray(v, dtype=np.float32)

    return (c(y[:SEQ])[None], c(y[SEQ:].reshape(DB, DS, D)),
            c(conv[:1])[None], c(dn[:1])[None], c(mc[:1])[None], c(mn[:1])[None], c(mm[:1])[None],
            c(hh[0][:1])[None], c(hh[1][:1])[None], c(mk)[None, None], c(mv)[None, None],
            c(conv[1:])[None], c(dn[1:])[None], c(mc[1:])[None], c(mn[1:])[None], c(mm[1:])[None],
            c(hh[0][1:])[None], c(hh[1][1:])[None])
```
